# Optimizing a Trainium2 kernel written in Bass

```python
import functools
import jax
import jax.numpy as jnp
from jax import lax
import numpy as np

D_MODEL = 1024
BATCH = 1
SEQ = 512
DEPTH = 1
DEC_BATCH = 8
DEC_SEQ = 8
PAST_LEN = 2048
PAGE_SIZE = 128

HEAD_DIM = 64
A_WINDOWS = (128, 512, 2048)
A_DILATIONS = (1, 4, 16)
A_GROUPS = 3
A_HEADS_PER_GROUP = 4
A_HEADS = A_GROUPS * A_HEADS_PER_GROUP
A_OUT = A_HEADS_PER_GROUP * HEAD_DIM
B_HEADS = 8
B_OUT = B_HEADS * HEAD_DIM
Q_BLOCK = 128
ROPE_THETA = 10000.0
RMS_EPS = 1e-6
FORGET_BIAS = 2.0
N_EXPERT_GROUPS = 4
EXPERTS_PER_GROUP = 8
INNER_TOP_K = 2
EXPERT_HIDDEN = 256
IN_SPLITS = (A_HEADS * HEAD_DIM, A_HEADS * HEAD_DIM, A_HEADS * HEAD_DIM, B_OUT, B_OUT, B_OUT, B_HEADS, D_MODEL, D_MODEL)
IN_WIDTH = sum(IN_SPLITS)

kernel_name = 'hybrid_dilated_fox_hmoe_step'

def rmsnorm(x, g):
    xf = x.astype(jnp.float32)
    y = xf * lax.rsqrt(jnp.mean(xf * xf, axis=-1, keepdims=True) + RMS_EPS)
    return (y * g.astype(jnp.float32)).astype(x.dtype)

def rope(x, pos):
    half = HEAD_DIM // 2
    inv_freq = ROPE_THETA ** (-jnp.arange(half, dtype=jnp.float32) / half)
    ang = pos.astype(jnp.float32)[:, None] * inv_freq[None, :]
    cos = jnp.cos(ang)[None, :, None, :]
    sin = jnp.sin(ang)[None, :, None, :]
    xf = x.astype(jnp.float32)
    x1, x2 = xf[..., :half], xf[..., half:]
    return jnp.concatenate([x1 * cos - x2 * sin, x2 * cos + x1 * sin], axis=-1).astype(x.dtype)

def adaln_terms(c, w_ada, b_ada):
    mod = jax.nn.silu(c) @ w_ada + b_ada
    return tuple(m[:, None, :] for m in jnp.split(mod, 6, axis=-1))

def mixer_inputs(h, w_in, b_f, pos):
    b, s, _ = h.shape
    proj = h @ w_in
    qa, ka, va, qb, kb, vb, fl, ga, gb = jnp.split(proj, np.cumsum(IN_SPLITS)[:-1].tolist(), axis=-1)
    qa = rope(qa.reshape(b, s, A_HEADS, HEAD_DIM), pos)
    ka = rope(ka.reshape(b, s, A_HEADS, HEAD_DIM), pos)
    va = va.reshape(b, s, A_HEADS, HEAD_DIM)
    qb = qb.reshape(b, s, B_HEADS, HEAD_DIM)
    kb = kb.reshape(b, s, B_HEADS, HEAD_DIM)
    vb = vb.reshape(b, s, B_HEADS, HEAD_DIM)
    logf = jax.nn.log_sigmoid(fl.astype(jnp.float32) + b_f.astype(jnp.float32))
    return qa, ka, va, qb, kb, vb, logf, jax.nn.sigmoid(ga), jax.nn.sigmoid(gb)

def head_group(t, g):
    return t[:, :, g * A_HEADS_PER_GROUP:(g + 1) * A_HEADS_PER_GROUP]

def masked_softmax_parts(s, valid):
    s = jnp.where(valid, s, -jnp.inf)
    m = jnp.max(s, axis=-1, keepdims=True)
    p = jnp.exp(s - m)
    den = jnp.sum(p, axis=-1)
    return p, den, m[..., 0] + jnp.log(den)

def dilated_window_prompt(q, k, v, window, dilation):
    b, s, h, e = q.shape
    wm = window // dilation
    n_str = s // dilation
    nblk = -(-n_str // wm)
    lp = nblk * wm

    def strided(t):
        t = t.reshape(b, n_str, dilation, h, e).transpose(0, 2, 1, 3, 4)
        t = jnp.pad(t, ((0, 0), (0, 0), (0, lp - n_str), (0, 0), (0, 0)))
        return t.reshape(b, dilation, nblk, wm, h, e)

    qs, ks, vs = strided(q), strided(k), strided(v)
    shift = ((0, 0), (0, 0), (1, 0), (0, 0), (0, 0), (0, 0))
    kk = jnp.concatenate([jnp.pad(ks, shift)[:, :, :-1], ks], axis=3)
    vv = jnp.concatenate([jnp.pad(vs, shift)[:, :, :-1], vs], axis=3)
    sc = jnp.einsum('brnqhe,brnkhe->brnhqk', qs, kk).astype(jnp.float32) * (e ** -0.5)
    qi = np.arange(wm)[:, None]
    kj = np.arange(2 * wm)[None, :]
    dist = wm + qi - kj
    key_pos = (np.arange(nblk)[:, None, None] - 1) * wm + kj[None]
    valid = (dist >= 0) & (dist <= wm) & (key_pos >= 0)
    p, den, lse = masked_softmax_parts(sc, valid[None, None, :, None])
    o = jnp.einsum('brnhqk,brnkhe->brnqhe', p, vv) / jnp.swapaxes(den, -1, -2)[..., None]
    o = o.reshape(b, dilation, lp, h, e)[:, :, :n_str].transpose(0, 2, 1, 3, 4).reshape(b, s, h, e)
    lse = jnp.swapaxes(lse, -1, -2).reshape(b, dilation, lp, h)[:, :, :n_str]
    lse = lse.transpose(0, 2, 1, 3).reshape(b, s, h)
    return o, lse

def dilated_window_sample(q, kv_buf, k_new, v_new, window, dilation):
    b, t, h, e = q.shape
    lw = kv_buf.shape[1]
    wm = window // dilation
    kv_all = jnp.concatenate([kv_buf, jnp.stack([k_new, v_new], axis=2)], axis=1)
    idx = lw + np.arange(t)[:, None] - dilation * np.arange(wm + 1)[None, :]
    valid = idx >= 0
    g = kv_all[:, np.maximum(idx, 0)]
    sc = jnp.einsum('bqhe,bqjhe->bhqj', q, g[:, :, :, 0]).astype(jnp.float32) * (e ** -0.5)
    p, den, lse = masked_softmax_parts(sc, valid[None, None])
    o = jnp.einsum('bhqj,bqjhe->bqhe', p, g[:, :, :, 1]) / jnp.swapaxes(den, 1, 2)[..., None]
    return o, jnp.swapaxes(lse, 1, 2), kv_all[:, t:]

def combine_by_denominator(outs, lses):
    w = jax.nn.softmax(jnp.stack(lses, axis=0), axis=0)
    return jnp.sum(w[..., None] * jnp.stack(outs, axis=0), axis=0)

def fox_prompt(q, k, v, logf):
    b, s, h, e = q.shape
    nblk = s // Q_BLOCK
    c = jnp.cumsum(logf.astype(jnp.float32), axis=1)
    c_keys = jnp.transpose(c, (0, 2, 1))[:, :, None, :]
    q_blocks = jnp.swapaxes(q.reshape(b, nblk, Q_BLOCK, h, e), 0, 1)
    c_blocks = jnp.swapaxes(c.reshape(b, nblk, Q_BLOCK, h), 0, 1)
    starts = jnp.arange(nblk) * Q_BLOCK
    key_pos = jnp.arange(s)

    def one_block(args):
        qi, ci, start = args
        sc = jnp.einsum('bqhe,bkhe->bhqk', qi, k).astype(jnp.float32) * (e ** -0.5)
        sc = sc + jnp.transpose(ci, (0, 2, 1))[..., None] - c_keys
        causal = key_pos[None, :] <= (start + jnp.arange(Q_BLOCK))[:, None]
        pr = jax.nn.softmax(jnp.where(causal, sc, -jnp.inf), axis=-1)
        return jnp.einsum('bhqk,bkhe->bqhe', pr, v)

    o = lax.map(one_block, (q_blocks, c_blocks, starts))
    return jnp.swapaxes(o, 0, 1).reshape(b, s, h, e)

def fox_sample(q, k_new, v_new, logf_new, k_past, v_past, logf_past):
    e = q.shape[-1]
    t = q.shape[1]
    n_past = k_past.shape[1]
    c_past = jnp.cumsum(logf_past.astype(jnp.float32), axis=1)
    c_new = c_past[:, -1:] + jnp.cumsum(logf_new.astype(jnp.float32), axis=1)
    cq = jnp.transpose(c_new, (0, 2, 1))[..., None]
    s_past = jnp.einsum('bqhe,bkhe->bhqk', q, k_past).astype(jnp.float32) * (e ** -0.5)
    s_past = s_past + cq - jnp.transpose(c_past, (0, 2, 1))[:, :, None, :]
    s_new = jnp.einsum('bqhe,bkhe->bhqk', q, k_new).astype(jnp.float32) * (e ** -0.5)
    s_new = s_new + cq - jnp.transpose(c_new, (0, 2, 1))[:, :, None, :]
    s_new = jnp.where(np.tril(np.ones((t, t), dtype=bool)), s_new, -jnp.inf)
    pr = jax.nn.softmax(jnp.concatenate([s_past, s_new], axis=-1), axis=-1)
    return (jnp.einsum('bhqk,bkhe->bqhe', pr[..., :n_past], v_past)
            + jnp.einsum('bhqk,bkhe->bqhe', pr[..., n_past:], v_new))

def merge_branches(oa, ob, ga, gb, w_pa, w_pb, w_o):
    b, s = oa.shape[:2]
    ya = oa.reshape(b, s, A_OUT) @ w_pa
    yb = ob.reshape(b, s, B_OUT) @ w_pb
    return (ga * ya + gb * yb) @ w_o

def hier_moe(h, w_rg, b_rg, w_re, b_re, w_eg, w_eu, w_ed):
    b, s, d = h.shape
    t = h.reshape(b * s, d)
    lg = (t @ w_rg).astype(jnp.float32) + b_rg
    pg = jax.nn.softmax(lg, axis=-1)
    onehot_g = jax.nn.one_hot(jnp.argmax(lg, axis=-1), N_EXPERT_GROUPS, dtype=jnp.float32)
    p_top = jnp.sum(pg * onehot_g, axis=-1, keepdims=True)
    le = jnp.einsum('nd,gde->nge', t, w_re).astype(jnp.float32) + b_re
    le_sel = jnp.sum(le * onehot_g[:, :, None], axis=1)
    top_v, top_i = lax.top_k(le_sel, INNER_TOP_K)
    w_top = jax.nn.softmax(top_v, axis=-1) * p_top
    inner = jnp.sum(jax.nn.one_hot(top_i, EXPERTS_PER_GROUP, dtype=jnp.float32) * w_top[..., None], axis=1)
    comb = onehot_g[:, :, None] * inner[:, None, :]
    out = jnp.zeros((b * s, d), jnp.float32)
    for g in range(N_EXPERT_GROUPS):
        a = jnp.einsum('nd,edf->nef', t, w_eg[g])
        u = jnp.einsum('nd,edf->nef', t, w_eu[g])
        act = jax.nn.silu(a) * u * comb[:, g, :, None].astype(t.dtype)
        out = out + jnp.einsum('nef,efd->nd', act, w_ed[g]).astype(jnp.float32)
    return out.reshape(b, s, d).astype(h.dtype)

def attend_prompt(qa, ka, va, qb, kb, vb, logf):
    s = qa.shape[1]
    outs, lses, bufs = [], [], []
    for g in range(A_GROUPS):
        qg, kg, vg = head_group(qa, g), head_group(ka, g), head_group(va, g)
        o, lse = dilated_window_prompt(qg, kg, vg, A_WINDOWS[g], A_DILATIONS[g])
        outs.append(o)
        lses.append(lse)
        keep = min(A_WINDOWS[g], s)
        bufs.append(jnp.stack([kg[:, s - keep:], vg[:, s - keep:]], axis=2))
    oa = combine_by_denominator(outs, lses)
    ob = fox_prompt(qb, kb, vb, logf)
    return oa, ob, (*bufs, kb, vb, logf)

def attend_sample(bufs_in, k_past, v_past, logf_past, qa, ka, va, qb, kb, vb, logf):
    outs, lses, bufs = [], [], []
    for g in range(A_GROUPS):
        o, lse, nb = dilated_window_sample(head_group(qa, g), bufs_in[g], head_group(ka, g),
                                           head_group(va, g), A_WINDOWS[g], A_DILATIONS[g])
        outs.append(o)
        lses.append(lse)
        bufs.append(nb)
    oa = combine_by_denominator(outs, lses)
    ob = fox_sample(qb, kb, vb, logf, k_past, v_past, logf_past)
    return oa, ob, (*bufs, kb, vb, logf)

def decoder_layer(x, c, pos, p, attend):
    sh1, sc1, gt1, sh2, sc2, gt2 = adaln_terms(c, p['w_ada'], p['b_ada'])
    h = rmsnorm(x, p['g_pre_mix']) * (1 + sc1) + sh1
    qa, ka, va, qb, kb, vb, logf, ga, gb = mixer_inputs(h, p['w_in'], p['b_f'], pos)
    oa, ob, state = attend(qa, ka, va, qb, kb, vb, logf)
    mix = merge_branches(oa.astype(x.dtype), ob.astype(x.dtype), ga, gb, p['w_pa'], p['w_pb'], p['w_o'])
    x = x + gt1 * rmsnorm(mix, p['g_post_mix'])
    h2 = rmsnorm(x, p['g_pre_ffn']) * (1 + sc2) + sh2
    ffn = hier_moe(h2, p['w_rg'], p['b_rg'], p['w_re'], p['b_re'], p['w_eg'], p['w_eu'], p['w_ed'])
    x = x + gt2 * rmsnorm(ffn, p['g_post_ffn'])
    return x, state

def setup_inputs(seed: int = 0) -> dict:
    key = jax.random.key(seed)
    ks = jax.random.split(key, 32)
    f32 = jnp.float32
    n_pages = PAST_LEN // PAGE_SIZE
    n_pool = (DEC_BATCH * n_pages * 5) // 4
    lw = [min(w, PAST_LEN) for w in A_WINDOWS]

    def nrm(k, shape, scale=1.0):
        return jax.random.normal(k, shape, f32) * scale

    G, E, F, D = N_EXPERT_GROUPS, EXPERTS_PER_GROUP, EXPERT_HIDDEN, D_MODEL
    page_table = jax.random.permutation(ks[8], n_pool)[:DEC_BATCH * n_pages]
    return {
        'x_prompt': nrm(ks[0], (BATCH, SEQ, D)),
        'x_sample': nrm(ks[1], (DEC_BATCH, DEC_SEQ, D)),
        'cache_a1_kv': nrm(ks[2], (DEPTH, DEC_BATCH, lw[0], 2, A_HEADS_PER_GROUP, HEAD_DIM)),
        'cache_a2_kv': nrm(ks[3], (DEPTH, DEC_BATCH, lw[1], 2, A_HEADS_PER_GROUP, HEAD_DIM)),
        'cache_a3_kv': nrm(ks[4], (DEPTH, DEC_BATCH, lw[2], 2, A_HEADS_PER_GROUP, HEAD_DIM)),
        'cache_b_k': nrm(ks[5], (DEPTH, n_pool, PAGE_SIZE, B_HEADS, HEAD_DIM)),
        'cache_b_v': nrm(ks[6], (DEPTH, n_pool, PAGE_SIZE, B_HEADS, HEAD_DIM)),
        'cache_b_logf': jax.nn.log_sigmoid(FORGET_BIAS + nrm(ks[7], (DEPTH, n_pool, PAGE_SIZE, B_HEADS))),
        'page_table': page_table.reshape(DEC_BATCH, n_pages).astype(jnp.int32),
        'c_prompt': nrm(ks[9], (BATCH, D)),
        'c_sample': nrm(ks[10], (DEC_BATCH, D)),
        'w_ada': nrm(ks[11], (DEPTH, D, 6 * D), 0.5 * D ** -0.5),
        'b_ada': nrm(ks[12], (DEPTH, 6 * D), 0.01),
        'g_pre_mix': 1.0 + nrm(ks[13], (DEPTH, D), 0.05),
        'g_post_mix': 1.0 + nrm(ks[14], (DEPTH, D), 0.05),
        'g_pre_ffn': 1.0 + nrm(ks[15], (DEPTH, D), 0.05),
        'g_post_ffn': 1.0 + nrm(ks[16], (DEPTH, D), 0.05),
        'w_in': nrm(ks[17], (DEPTH, D, IN_WIDTH), D ** -0.5),
        'b_f': FORGET_BIAS + nrm(ks[18], (DEPTH, B_HEADS), 0.1),
        'w_pa': nrm(ks[19], (DEPTH, A_OUT, D), A_OUT ** -0.5),
        'w_pb': nrm(ks[20], (DEPTH, B_OUT, D), B_OUT ** -0.5),
        'w_o': nrm(ks[21], (DEPTH, D, D), D ** -0.5),
        'w_router_group': nrm(ks[22], (DEPTH, D, G), D ** -0.5),
        'b_router_group': nrm(ks[23], (DEPTH, G), 0.01),
        'w_router_expert': nrm(ks[24], (DEPTH, G, D, E), D ** -0.5),
        'b_router_expert': nrm(ks[25], (DEPTH, G, E), 0.01),
        'w_exp_gate': nrm(ks[26], (DEPTH, G, E, D, F), D ** -0.5),
        'w_exp_up': nrm(ks[27], (DEPTH, G, E, D, F), D ** -0.5),
        'w_exp_down': nrm(ks[28], (DEPTH, G, E, F, D), F ** -0.5),
    }

def reference(x_prompt, x_sample, cache_a1_kv, cache_a2_kv, cache_a3_kv, cache_b_k, cache_b_v, cache_b_logf,
              page_table, c_prompt, c_sample, w_ada, b_ada, g_pre_mix, g_post_mix, g_pre_ffn, g_post_ffn,
              w_in, b_f, w_pa, w_pb, w_o, w_router_group, b_router_group, w_router_expert, b_router_expert,
              w_exp_gate, w_exp_up, w_exp_down):
    n_seq, n_pages = page_table.shape
    past = n_pages * PAGE_SIZE
    pos_prompt = jnp.arange(x_prompt.shape[1])
    pos_sample = past + jnp.arange(x_sample.shape[1])
    y_prompt, y_sample = x_prompt, x_sample
    st_prompt, st_sample = [], []
    for layer in range(DEPTH):
        p = {
            'w_ada': w_ada[layer], 'b_ada': b_ada[layer],
            'g_pre_mix': g_pre_mix[layer], 'g_post_mix': g_post_mix[layer],
            'g_pre_ffn': g_pre_ffn[layer], 'g_post_ffn': g_post_ffn[layer],
            'w_in': w_in[layer], 'b_f': b_f[layer],
            'w_pa': w_pa[layer], 'w_pb': w_pb[layer], 'w_o': w_o[layer],
            'w_rg': w_router_group[layer], 'b_rg': b_router_group[layer],
            'w_re': w_router_expert[layer], 'b_re': b_router_expert[layer],
            'w_eg': w_exp_gate[layer], 'w_eu': w_exp_up[layer], 'w_ed': w_exp_down[layer],
        }
        y_prompt, sp = decoder_layer(y_prompt, c_prompt, pos_prompt, p, attend_prompt)
        k_past = cache_b_k[layer, page_table].reshape(n_seq, past, B_HEADS, HEAD_DIM)
        v_past = cache_b_v[layer, page_table].reshape(n_seq, past, B_HEADS, HEAD_DIM)
        lf_past = cache_b_logf[layer, page_table].reshape(n_seq, past, B_HEADS)
        attend = functools.partial(attend_sample, (cache_a1_kv[layer], cache_a2_kv[layer], cache_a3_kv[layer]),
                                   k_past, v_past, lf_past)
        y_sample, ss = decoder_layer(y_sample, c_sample, pos_sample, p, attend)
        st_prompt.append(sp)
        st_sample.append(ss)
    a1_prompt, a2_prompt, a3_prompt, bk_prompt, bv_prompt, blogf_prompt = [
        jnp.stack(t, axis=0) for t in zip(*st_prompt)]
    a1_sample, a2_sample, a3_sample, bk_sample, bv_sample, blogf_sample = [
        jnp.stack(t, axis=0) for t in zip(*st_sample)]
    return (y_prompt, y_sample, a1_prompt, a1_sample, a2_prompt, a2_sample, a3_prompt, a3_sample,
            bk_prompt, bk_sample, bv_prompt, bv_sample, blogf_prompt, blogf_sample)


_drawn_inputs = setup_inputs


def setup_inputs(seed=0):
    import zlib

    import numpy as np

    out = dict(_drawn_inputs(seed))
    spreads = {}
    factors = {'g_post_ffn': 4.033, 'b_router_expert': 2.871}
    for name, (base, spread) in spreads.items():
        noise = np.random.default_rng([zlib.crc32(name.encode()), seed]).standard_normal(out[name].shape)
        drawn = base * np.exp(spread * noise) if base else spread * noise
        out[name] = jnp.asarray(drawn.astype(out[name].dtype))
    for name, factor in factors.items():
        out[name] = (out[name] * factor).astype(out[name].dtype)
    return out
```

```python
import numpy as np
import concourse.bass as bass
from concourse import mybir
from concourse.alu_op_type import AluOpType as ALU
from contextlib import ExitStack

F32 = mybir.dt.float32
I32 = mybir.dt.int32
U32 = mybir.dt.uint32
ACT = mybir.ActivationFunctionType
AX = mybir.AxisListType.X
ds = bass.ds

P = 128
D = 1024
KD = D // P
SEQ, NSEQ, DEC = 512, 8, 8
NS = NSEQ * DEC
NT = SEQ + NS
TILES = SEQ // P + 1
ROWS = [P] * (TILES - 1) + [NS]
PAST, PAGE = 2048, 128
PAGES = PAST // PAGE
POOL = 5 * NSEQ * PAGES // 4
HD = 64
GROUPS, AH, BH = 3, 4, 8
AW, BW = GROUPS * AH * HD, BH * HD
QA, KA, VA = 0, AW, 2 * AW
QB, KB, VB = 3 * AW, 3 * AW + BW, 3 * AW + 2 * BW
FL = 3 * AW + 3 * BW
QKV = FL + BH
CH = 8
CW = QKV // CH
ADA = 6 * D // 512
ADA_A = 4
EPS = 1e-6
SCALE = HD ** -0.5
NEG = -1e30
WIN = (128, 512, 2048)
DIL = (1, 4, 16)
BUFROWS = [min(w, PAST) for w in WIN]
NG, NE, TOPK, HID = 4, 8, 2, 256
EXPERTS = NG * NE
SLOTS = 64
OVER = NT * TOPK // SLOTS
BLOCKS = EXPERTS + OVER
EXPERT_W = (2 * HID * D + HID * D) // P
RING = 4


class Link:

    def __init__(self, eng, sem):
        self.eng, self.sem, self.n, self.loop = eng, sem, 0, 0

    def __call__(self, ins):
        self.n += 1
        ins.then_inc(self.sem, 1)
        self.eng.wait_ge(self.sem, self.loop + self.n)



class Memory:

    def weights(self, b):
        u = (b + 2) % RING
        return self.w[:, u * EXPERT_W:(u + 1) * EXPERT_W]


def build(nc, I, O):
    with ExitStack() as ctx:
        m = Memory()
        m.sb = lambda name, shape, dt=F32: ctx.enter_context(nc.sbuf_tensor(name, shape, dt))
        m.ident = m.sb("ident", [P, P])
        m.mod = m.sb("mod", [P, ADA // 4, 512])
        m.sel = m.sb("sel", [P, P + NS])
        m.mp = m.sb("mp", [P, 3, D])
        m.ms = m.sb("ms", [NS, 3, D])
        m.hT = m.sb("hT", [P, KD, NT])
        m.oaT = m.sb("oaT", [P, 2, NT])
        m.obT = m.sb("obT", [P, 4, NT])
        m.banks = [ctx.enter_context(nc.psum_tensor(f"bank{b}", [P, 512], F32)) for b in range(8)]
        m.h2 = nc.dram_tensor("h2", (NT, D), F32, kind="Internal").ap()
        m.y = nc.dram_tensor("y", (BLOCKS * SLOTS, D), F32, kind="Internal").ap()
        m.table = nc.dram_tensor("table", (SLOTS, BLOCKS), I32, kind="Internal").ap()
        m.s_keep = ctx.enter_context(nc.semaphore("window_copied"))
        with ExitStack() as attn:
            sa = lambda name, shape, dt=F32: attn.enter_context(nc.sbuf_tensor(name, shape, dt))
            m.q_b = sa("q_b", [P, 4, NSEQ, BH * DEC])
            m.q_a = sa("q_a", [P, 2 * GROUPS, NSEQ, AH * DEC])
            m.kn_b = sa("kn_b", [P, 4, NS])
            m.kn_a = sa("kn_a", [P, 2 * GROUPS, NS])
            m.vn = sa("vn", [NS, AW + BW])
            m.lfn = sa("lfn", [NS, BH])
            with ExitStack() as proj:
                sp_ = lambda name, shape, dt=F32: proj.enter_context(nc.sbuf_tensor(name, shape, dt))
                m.qkv = sp_("qkv", [P, TILES, QKV])
                m.logf = sp_("logf", [P, TILES, BH])
                m.st = sp_("silu_cond", [P, KD, 32])
                phase_a(nc, I, O, m)
                phase_b(nc, I, O, m)
            phase_c(nc, I, O, m)
        m.w = m.sb("w_expert", [P, RING * EXPERT_W])
        m.w_in = [ctx.enter_context(nc.semaphore(f"w_expert_in{u}")) for u in range(RING)]
        m.x1 = m.sb("x1", [P, TILES, D])
        m.wt = m.sb("weights", [P, TILES, TOPK])
        m.posy = m.sb("y_rows", [P, TILES, TOPK], I32)
        m.ownf = m.sb("owner_f", [1, OVER + 1])
        m.owni = m.sb("owner", [1, OVER + 1], I32)
        phase_d(nc, I, O, m)
        phase_e(nc, I, O, m)
        phase_f(nc, I, O, m)


def constants():
    sel = np.zeros((P, P + NS), np.float32)
    for j in range(4):
        sel[32 * j, 0:P] = 1.0
        for s in range(NSEQ):
            sel[32 * j + 1 + s, P + s * DEC:P + (s + 1) * DEC] = 1.0
    half = HD // 2
    inv = (np.float32(10000.0) ** (-np.arange(half, dtype=np.float32) / np.float32(half))).astype(np.float32)
    pos = np.zeros(TILES * P, np.float32)
    pos[0:SEQ] = np.arange(SEQ)
    pos[SEQ:NT] = PAST + np.tile(np.arange(DEC), NSEQ)
    ang = (pos[:, None] * inv[None, :]).astype(np.float32).astype(np.float64)
    rope = np.stack([np.cos(ang), np.sin(ang)], 1).astype(np.float32).reshape(TILES, P, 2, half).transpose(1, 0, 2, 3)
    q, k = np.arange(P)[:, None], np.arange(P)[None, :]
    no = lambda ok: np.where(ok, 0.0, NEG).astype(np.float32)
    parts = [no(k >= q), no(k <= q)]
    for dil in DIL[1:]:
        parts += [no((q - k) % dil == 0)] * 3 + [no(((q - k) % dil == 0) & (k <= q))]
    masks_prompt = np.concatenate(parts, axis=1)
    tri = np.concatenate([(q <= k).astype(np.float32), np.ones((P, SEQ - P), np.float32)], axis=1)
    t = np.tile(np.arange(DEC), AH)[:, None]
    j = np.arange(P)[None, :]
    window = [no((t % 4 == c) & (4 * j + c >= t)) for c in range(4)]
    window += [no((t == c) & (j >= 0)) for c in range(8)] + [no(j >= t)]
    tb = np.tile(np.arange(DEC), BH)[:, None]
    kn = np.arange(NS)[None, :] % DEC
    new_mask = np.zeros((BH * DEC + AH * DEC, NS), np.float32)
    new_mask[:BH * DEC] = no(kn <= tb)
    k8 = np.arange(DEC)[None, :]
    for g, dil in enumerate(DIL):
        new_mask[BH * DEC:, g * DEC:(g + 1) * DEC] = no((k8 <= t) & ((t - k8) % dil == 0))
    head_mask = np.zeros((BH * DEC + AH * DEC, BW), np.float32)
    for h in range(BH):
        head_mask[h * DEC:(h + 1) * DEC, h * HD:(h + 1) * HD] = 1.0
    for h in range(AH):
        head_mask[(BH + h) * DEC:(BH + h + 1) * DEC, h * HD:(h + 1) * HD] = 1.0
    fold = np.tile(np.eye(DEC, dtype=np.float32), (BH + AH, 1))
    pg, col = np.arange(P)[:, None], np.arange(P)[None, :]
    before = ((pg // PAGES == col // PAGES) & (pg < col)).astype(np.float32)
    r = np.arange(NS)
    seq_of = (pg // PAGES == r[None, :] // DEC).astype(np.float32)
    tri8 = np.zeros((P, NS), np.float32)
    tri8[:NS] = (r[:, None] // DEC == r[None, :] // DEC) & (r[:, None] <= r[None, :])
    strict = (pg < col).astype(np.float32)
    valid = np.ones((P, TILES), np.float32)
    valid[NS:, TILES - 1] = 0.0
    row_ids = (np.arange(TILES)[None, :] * P + np.arange(P)[:, None]).astype(np.int32)
    return {"rank_consts": np.concatenate([strict, np.ones((P, P), np.float32)], axis=1),
            "iota": np.tile(np.arange(EXPERTS, dtype=np.float32), (P, 1)), "row_ids": row_ids, "valid": valid,
            "over_ids": np.arange(EXPERTS, BLOCKS, dtype=np.float32)[None, :],
            "mask_window": np.concatenate(window, axis=1), "new_mask": new_mask, "head_mask": head_mask, "fold": fold,
            "page_consts": np.concatenate([before, seq_of, tri8], axis=1),
            "masks_prompt": masks_prompt, "tri": tri,
            "ident": np.eye(P, dtype=np.float32), "sel": sel, "rope": rope}


def spread_steps(m, terms, ready, freed):
    steps = [(slot, c0 + half, half, g, new) for slot, c0, g in terms for half in range(2) for new in range(2)]

    def tensor(nc, pe):
        for n, (slot, c, half, g, new) in enumerate(steps):
            if n >= 4:
                pe.wait_ge(freed, n - 3)
            j = 32 * (c % 4)
            lo, hi = (P, P + NS) if new else (0, P)
            nc.tensor.matmul(m.banks[4 + n % 4][0:hi - lo, :], m.sel[j:j + 32, lo:hi],
                             m.mod[j:j + 32, c // 4, :], start=True, stop=True).then_inc(ready, 1)

    def vector(nc, dve):
        for n, (slot, c, half, g, new) in enumerate(steps):
            dve.wait_ge(ready, n + 1)
            rows, dst = (NS, m.ms) if new else (P, m.mp)
            out = dst[0:rows, slot, half * 512:half * 512 + 512]
            src = m.banks[4 + n % 4][0:rows, :]
            if g is None:
                nc.vector.tensor_copy(out, src).then_inc(freed, 1)
            else:
                nc.vector.scalar_tensor_tensor(out, src, 1.0 if slot == 0 else 0.0,
                                               g[0:rows, half * 512:half * 512 + 512],
                                               ALU.add, ALU.mult).then_inc(freed, 1)

    return tensor, vector, len(steps)


def scale_of(m, i, slot):
    return m.mp[:, slot, :] if i < TILES - 1 else m.ms[:, slot, :]


def parts(i, width):
    return ((0, width, 0),) if ROWS[i] > P // 2 else ((0, width // 2, 0), (width // 2, width, P // 2))


def phase_a(nc, I, O, m):
    with ExitStack() as ctx:
        sb = lambda name, shape, dt=F32: ctx.enter_context(nc.sbuf_tensor(name, shape, dt))
        used = []

        def sem(name):
            used.append(ctx.enter_context(nc.semaphore("a_" + name)))
            return used[-1]
        RING = 2
        ring = sb("w_ring", [P, RING, KD * 512])
        ct = sb("ct", [P, KD, 32])
        st = m.st
        gain = sb("gain", [P, D])
        brow = sb("brow", [P, ADA // 4, 512])
        rope = sb("rope", [P, TILES, 2, HD // 2])
        bf = sb("bf", [P, BH])
        ssq = sb("ssq", [P, 3, TILES])
        lt = sb("lt", [P, 4, TILES * BH])
        x = m.qkv[:, :, 0:D]
        sq = m.qkv[:, :, D:2 * D]
        t1 = brow[:, :, :].rearrange("p a n -> p (a n)")[:, 0:AW].rearrange("p (h e) -> p h e", e=HD // 2)
        t2 = brow[:, :, :].rearrange("p a n -> p (a n)")[:, AW:2 * AW].rearrange("p (h e) -> p h e", e=HD // 2)
        con, cond, rows_in, gain_in, bias_in, rope_in = [sem(n) for n in ("const", "cond", "rows", "gain", "bias", "rope")]
        chunk_in = [sem(f"chunk{b}") for b in range(RING)]
        silu, ada, mod_out, spread, spread_out = [sem(n) for n in ("silu", "ada", "mod_out", "spread", "spread_out")]
        sum_sq, rstd, normed, row_h, turned, hT_d, hT_a = [sem(n) for n in (
            "sum_sq", "rstd", "normed", "row_h", "turned", "hT_dve", "hT_act")]
        zeros, y_fill = sem("zeros"), sem("y_fill")
        zero_rows = m.obT[0:SLOTS, :, :].rearrange("p a n -> p (a n)")[:, 0:D]
        proj, out_d, out_a = sem("proj"), sem("proj_dve"), sem("proj_act")
        dve_own, act_own, sin_part, cos_part, pool_half, dve_half = [sem(n) for n in (
            "dve_own", "act_own", "sin_part", "cos_part", "pool_half", "dve_half")]
        lg_in, lg_exp, lg_ln = sem("lg_in"), sem("lg_exp"), sem("lg_ln")
        block = ctx.enter_context(nc.Block(no_gpsimd_drain=True))
        last = TILES - 1
        assert CH == NSEQ
        m.finished = used
        ROPE_AFTER = 4
        assert ROPE_AFTER * CW >= 2 * AW
        spread_pe, spread_dve, SPREAD = spread_steps(m, [(0, 2, gain), (1, 0, None)], spread, spread_out)

        @block.sync
        def _(sp):
            sp.dma_start(ct[:], I["cond"]).then_inc(cond, 16)
            for n in range(ADA_A + CH):
                if n >= RING:
                    if n - RING < ADA_A:
                        sp.wait_ge(ada, n - RING + 1)
                    else:
                        sp.wait_ge(proj, TILES * (n - RING - ADA_A + 1))
                if n < ADA_A:
                    sp.dma_start(ring[:, n % RING, :], I["w_ada"][n]).then_inc(chunk_in[n % RING], 16)
                else:
                    sp.dma_start(ring[:, n % RING, 0:KD * CW], I["w_qkv"][n - ADA_A]).then_inc(chunk_in[n % RING], 16)
                    s = n - ADA_A
                    for g in range(GROUPS):
                        keep = BUFROWS[g] - DEC
                        sp.dma_start(O[f"a{g + 1}_sample"][s, 0:keep, :], I[f"cache_a{g + 1}"][s, DEC:DEC + keep, :]).then_inc(m.s_keep, 16)
                    sp.wait_ge(zeros, 1)
                    for j in range(s * OVER // CH, (s + 1) * OVER // CH):
                        sp.dma_start(m.y[(EXPERTS + j) * SLOTS:(EXPERTS + j + 1) * SLOTS, :], zero_rows).then_inc(y_fill, 16)
                if n == 1:
                    for j in range(4):
                        sp.dma_start(brow[32 * j:32 * j + 32, 0, :], I["b_ada"][j, 0].partition_broadcast(32)).then_inc(bias_in, 16)
                        sp.dma_start(m.mod[32 * j:32 * j + 32, 1:ADA // 4, :], I["b_ada"][j, 1:ADA // 4].partition_broadcast(32)).then_inc(bias_in, 16)
                    for i in range(TILES):
                        src = I["x_prompt"][i * P:(i + 1) * P, :] if i < last else I["x_sample"]
                        sp.dma_start(x[0:ROWS[i], i, :], src).then_inc(rows_in, 16)
                    sp.dma_start(m.sel[:], I["sel"]).then_inc(con, 16)
                    sp.dma_start(m.ident[:], I["ident"]).then_inc(con, 16)
                    sp.dma_start(gain[:], I["g_pre_mix"].partition_broadcast(P)).then_inc(gain_in, 16)
                    sp.dma_start(bf[:], I["b_f"].partition_broadcast(P)).then_inc(rope_in, 16)
                    sp.dma_start(rope[:], I["rope"]).then_inc(rope_in, 16)

            sp.wait_ge(y_fill, 16 * OVER)

        @block.tensor
        def _(pe):
            pe.wait_ge(silu, 2)
            for u in range(ADA_A):
                pe.wait_ge(chunk_in[u % RING], 16 * (u // RING + 1))
                for k in range(KD):
                    mm = nc.tensor.matmul(m.banks[u][32 * u:32 * u + 32, :], st[:, k, :], ring[:, u % RING, 512 * k:512 * k + 512],
                                          start=k == 0, stop=k == KD - 1)
                mm.then_inc(ada, 1)
            pe.wait_ge(con, 32)
            pe.wait_ge(mod_out, ADA_A)
            spread_pe(nc, pe)
            for i in range(TILES):
                pe.wait_ge(row_h, i + 1)
                for b in range(2):
                    if i >= 2:
                        pe.wait_ge(hT_a if b else hT_d, i - 1)
                    for k in range(4):
                        mm = nc.tensor.transpose(m.banks[2 * (i % 2) + b][:, k * P:k * P + ROWS[i]],
                                                 x[0:ROWS[i], i, (4 * b + k) * P:(4 * b + k + 1) * P],
                                                 m.ident[0:ROWS[i], 0:ROWS[i]])
                    mm.then_inc(turned, 1)
            pe.wait_ge(hT_d, TILES)
            pe.wait_ge(hT_a, TILES)
            with pe.Fori(0, CH // 2) as c2:
                for u in range(2):
                    pe.wait_ge(chunk_in[u], c2 * 16 + 16 * (ADA_A // RING + 1))
                    for i in range(TILES):
                        if i % 2:
                            pe.wait_ge(out_a, c2 * 4 + 2 * u + i // 2 + 1)
                        else:
                            pe.wait_ge(out_d, c2 * 6 + 3 * u + i // 2 + 1)
                        for k in range(KD):
                            for lo, hi, r in parts(i, CW):
                                mm = nc.tensor.matmul(m.banks[i][r:r + ROWS[i], 0:hi - lo], m.hT[:, k, i * P:i * P + ROWS[i]],
                                                      ring[:, u, CW * k + lo:CW * k + hi], start=k == 0, stop=k == KD - 1)
                        mm.then_inc(proj, 1)

        @block.scalar
        def _(act):
            act.sem_inc(out_a, 2)
            own = Link(act, act_own)
            act.wait_ge(cond, 16)
            own(nc.scalar.activation(st[:], ct[:], ACT.Exp, scale=-1.0))
            act.sem_inc(silu, 1)
            act.wait_ge(silu, 2)
            act.wait_ge(rows_in, 16 * TILES)
            for i in range(TILES):
                nc.scalar.activation(sq[0:ROWS[i], i, :], x[0:ROWS[i], i, :], ACT.Square,
                                     accum_out=ssq[0:ROWS[i], 0, i:i + 1]).then_inc(sum_sq, 1)
            act.wait_ge(rstd, 1)
            own(nc.scalar.activation(ssq[:, 1, :], ssq[:, 1, :], ACT.Ln))
            nc.scalar.activation(ssq[:, 2, :], ssq[:, 1, :], ACT.Exp, scale=-0.5).then_inc(rstd, 1)
            for i in range(TILES):
                act.wait_ge(turned, 2 * i + 2)
                nc.scalar.activation(m.hT[:, 4:8, i * P:i * P + ROWS[i]],
                                     m.banks[2 * (i % 2) + 1][:, :].rearrange("p (k r) -> p k r", r=P)[:, :, 0:ROWS[i]],
                                     ACT.Copy).then_inc(hT_a, 1)
            with act.Fori(0, CH) as c:
                for i in range(1, TILES, 2):
                    act.wait_ge(proj, c * TILES + i + 1)
                    nc.scalar.activation(m.qkv[:, i, ds(c * CW, CW)], m.banks[i][:, 0:CW], ACT.Copy).then_inc(out_a, 1)
            act.wait_ge(lg_in, 1)
            own(nc.scalar.activation(lt[:, 2, :], lt[:, 1, :], ACT.Exp, scale=-1.0))
            nc.scalar.activation(lt[:, 3, :], lt[:, 2, :], ACT.Ln, bias=1.0).then_inc(lg_ln, 1)

        @block.gpsimd
        def _(pool):
            nc.gpsimd.memset(zero_rows, 0.0).then_inc(zeros, 1)
            for i in range(TILES):
                pool.wait_ge(normed, i + 1)
                xi = x[0:ROWS[i], i, :]
                nc.gpsimd.tensor_tensor(xi, xi, scale_of(m, i, 1)[0:ROWS[i]], ALU.add).then_inc(row_h, 1)
            pool.wait_ge(rope_in, 32)
            for n in range(2 * TILES):
                i, part = n // 2, n % 2
                z = m.qkv[0:ROWS[i], i, part * AW:(part + 1) * AW].rearrange("p (h e) -> p h e", e=HD // 2)
                if n % 2 == 0:
                    pool.wait_ge(out_d, 3 * (ROPE_AFTER + 1))
                    pool.wait_ge(out_a, 2 * (ROPE_AFTER + 1))
                if n >= 1:
                    pool.wait_ge(dve_half, n)
                    pool.wait_ge(pool_half, n)
                sin = rope[0:ROWS[i], i, 1:2, :].to_broadcast([ROWS[i], AW // 32, HD // 2])
                nc.gpsimd.tensor_tensor(t2[0:ROWS[i]], z, sin, ALU.mult).then_inc(sin_part, 1)
                pool.wait_ge(sin_part, n + 1)
                pool.wait_ge(cos_part, n + 1)
                pr = lambda a, b: a.rearrange("p (h b) e -> p h b e", b=2)[:, :, b, :]
                nc.gpsimd.tensor_tensor(pr(z, 1), pr(t1[0:ROWS[i]], 1), pr(t2[0:ROWS[i]], 0), ALU.add).then_inc(pool_half, 1)
            pool.wait_ge(pool_half, 2 * TILES)

        @block.vector
        def _(dve):
            own = Link(dve, dve_own)
            dve.sem_inc(out_d, 3)
            own(nc.vector.memset(ssq[:, 0, :], 0.0))
            dve.wait_ge(silu, 1)
            own(nc.vector.tensor_scalar(st[:], st[:], 1.0, None, ALU.add))
            own(nc.vector.reciprocal(st[:], st[:]))
            nc.vector.tensor_tensor(st[:], st[:], ct[:], ALU.mult).then_inc(silu, 1)
            dve.wait_ge(bias_in, 128)
            for u in range(ADA_A):
                dve.wait_ge(ada, u + 1)
                nc.vector.tensor_tensor(m.mod[32 * u:32 * u + 32, 0, :], m.banks[u][32 * u:32 * u + 32, :],
                                        brow[32 * u:32 * u + 32, 0, :], ALU.add).then_inc(mod_out, 1)
            dve.wait_ge(sum_sq, TILES)
            own(nc.vector.tensor_scalar(ssq[:, 1, :], ssq[:, 0, :], 1.0 / D, EPS, ALU.mult, ALU.add))
            dve.sem_inc(rstd, 1)
            dve.wait_ge(gain_in, 16)
            spread_dve(nc, dve)
            dve.wait_ge(spread_out, SPREAD)
            dve.wait_ge(rstd, 2)
            for i in range(TILES):
                xi = x[0:ROWS[i], i, :]
                nc.vector.scalar_tensor_tensor(xi, xi, ssq[0:ROWS[i], 2, i:i + 1], scale_of(m, i, 0)[0:ROWS[i]],
                                               ALU.mult, ALU.mult).then_inc(normed, 1)
            for i in range(TILES):
                dve.wait_ge(turned, 2 * i + 1)
                nc.vector.tensor_copy(m.hT[:, 0:4, i * P:i * P + ROWS[i]],
                                      m.banks[2 * (i % 2)][:, :].rearrange("p (k r) -> p k r", r=P)[:, :, 0:ROWS[i]]).then_inc(hT_d, 1)

            def copy_out(c):
                for i in range(0, TILES, 2):
                    dve.wait_ge(proj, c * TILES + i + 1)
                    for lo, hi, r in parts(i, CW):
                        ins = nc.vector.tensor_copy(m.qkv[0:ROWS[i], i, ds(c * CW + lo, hi - lo)], m.banks[i][r:r + ROWS[i], 0:hi - lo])
                    ins.then_inc(out_d, 1)

            def rotate(n):
                i, part = n // 2, n % 2
                z = m.qkv[0:ROWS[i], i, part * AW:(part + 1) * AW].rearrange("p (h e) -> p h e", e=HD // 2)
                pr = lambda a, b: a.rearrange("p (h b) e -> p h b e", b=2)[:, :, b, :]
                cos = rope[0:ROWS[i], i, 0:1, :].to_broadcast([ROWS[i], AW // 32, HD // 2])
                if n >= 1:
                    dve.wait_ge(pool_half, n)
                    dve.wait_ge(dve_half, n)
                nc.vector.tensor_tensor(t1[0:ROWS[i]], z, cos, ALU.mult).then_inc(cos_part, 1)
                dve.wait_ge(cos_part, n + 1)
                dve.wait_ge(sin_part, n + 1)
                nc.vector.tensor_tensor(pr(z, 0), pr(t1[0:ROWS[i]], 0), pr(t2[0:ROWS[i]], 1), ALU.subtract).then_inc(dve_half, 1)

            with dve.Fori(0, ROPE_AFTER) as c:
                copy_out(c)
            dve.wait_ge(rope_in, 32)
            dve.wait_ge(out_d, 3 * (ROPE_AFTER + 1))
            dve.wait_ge(out_a, 2 * (ROPE_AFTER + 1))
            for c in range(ROPE_AFTER, CH):
                for n in range(3 * (c - ROPE_AFTER), min(3 * (c - ROPE_AFTER) + 3, 2 * TILES)):
                    rotate(n)
                copy_out(c)
            dve.wait_ge(out_d, 3 * (CH + 1))
            dve.wait_ge(out_a, 2 * (CH + 1))
            z = lt[:, 0, :].rearrange("p (i h) -> p i h", h=BH)
            own(nc.vector.memset(lt[:, 0, :], 0.0))
            for lo, hi, rows in ((0, last, P), (last, TILES, NS)):
                o = nc.vector.tensor_tensor(z[0:rows, lo:hi, :], m.qkv[0:rows, lo:hi, FL:QKV],
                                            bf[0:rows].unsqueeze(1).to_broadcast([rows, hi - lo, BH]), ALU.add)
                own(o)
            own(nc.vector.tensor_scalar(lt[:, 1, :], lt[:, 0, :], -1.0, None, ALU.mult))
            own(nc.vector.tensor_tensor(lt[:, 1, :], lt[:, 0, :], lt[:, 1, :], ALU.max))
            dve.sem_inc(lg_in, 1)
            dve.wait_ge(lg_ln, 1)
            nc.vector.scalar_tensor_tensor(m.logf[:, :, :].rearrange("p i h -> p (i h)"), lt[:, 0, :], 0.0, lt[:, 3, :],
                                           ALU.min, ALU.subtract).then_inc(dve_own, 1)
            dve.wait_ge(dve_own, own.n + 1)
            dve.wait_ge(dve_half, 2 * TILES)


def phase_b(nc, I, O, m):
    with ExitStack() as ctx:
        sb = lambda name, shape, dt=F32: ctx.enter_context(nc.sbuf_tensor(name, shape, dt))

        def sem(name):
            m.finished.append(ctx.enter_context(nc.semaphore("b_" + name)))
            return m.finished[-1]
        qk_b = sb("qk_b", [P, 2, 2, SEQ])
        both = sb("bias_or_qk", [P, BH * SEQ])
        cb = both[:, :].rearrange("p (h k) -> p h k", k=SEQ)
        qk_a = both[:, 0:6 * SEQ].rearrange("p (a k) -> p a k", k=SEQ)
        WIDE = 3
        masks = m.obT[:, :, :].rearrange("p a n -> p (a n)")[:, 0:256 + 512 + 512]
        sbuf = sb("scores", [P, WIDE * 1280])
        pt = sb("probs_t", [P, 3, 512])
        tri = pt[:, 2, :]
        UNITS = []
        for h in range(BH):
            for i in range(4):
                UNITS.append(dict(kind="b", h=h, i=i, rnd=h // 2))
        for h in range(AH):
            for i in range(4):
                UNITS.append(dict(kind="a", h=h, i=i, rnd=4 + h // 2))
        nmax = sb("nmax", [P, len(UNITS)])
        den = sb("den", [P, 2, len(UNITS)])

        seg = blk = 0
        free_bank = {}
        for u, t in enumerate(UNITS):
            h, i = t["h"], t["i"]
            r = 64 * (h % 2)
            rows = slice(r, r + 64)
            segs, v = [], []
            if t["kind"] == "b":
                n = P * (i + 1)
                par = t["rnd"] % 2
                t["at"] = 512 * (u % 6)
                segs.append((u % 3, qk_b[rows, par, 0, i * P:(i + 1) * P], qk_b[rows, par, 1, 0:n], 0, n))
                v = [m.qkv[:, b, VB + HD * h:VB + HD * h + HD] for b in range(i + 1)]
                t["out"] = m.qkv[:, i, QB + HD * h:QB + HD * h + HD]
            else:
                t["at"] = 1280 * (u % WIDE)
                off = 0
                for g in range(GROUPS):
                    b0 = max(i - 1, 0) if g == 0 else 0
                    n = P * (i + 1 - b0)
                    segs.append((g, qk_a[rows, 2 * g, i * P:(i + 1) * P], qk_a[rows, 2 * g + 1, b0 * P:b0 * P + n], off, n))
                    off += n
                    c = VA + HD * (AH * g + h)
                    v += [m.qkv[:, b, c:c + HD] for b in range(b0, i + 1)]
                t["out"] = m.qkv[:, i, QA + HD * h:QA + HD * h + HD]
            t["segs"], t["v"] = segs, v
            t["seg0"], t["width"] = seg, P * len(v)
            seg += len(segs)
            t["groups"] = [(b, min(4, len(v) - b)) for b in range(0, len(v), 4)]
            t["grp0"] = blk
            blk += len(t["groups"])
            t["bank_free"] = [free_bank.get(s[0], 0) for s in segs]
            for k, s in enumerate(segs):
                free_bank[s[0]] = t["seg0"] + k + 1
            lo, hi = t["at"], t["at"] + t["width"]
            t["buf_free"] = max([w["grp0"] + len(w["groups"]) for w in UNITS[:u] if w["at"] < hi and lo < w["at"] + w["width"]], default=0)
        SETS = []
        for rnd in range(4):
            SETS += [(rnd, QB + P * rnd, qk_b[:, rnd % 2, 0, :]), (rnd, KB + P * rnd, qk_b[:, rnd % 2, 1, :])]
        for hp in range(2):
            for g in range(GROUPS):
                c = HD * (AH * g + 2 * hp)
                SETS += [(4 + hp, QA + c, qk_a[:, 2 * g, :]), (4 + hp, KA + c, qk_a[:, 2 * g + 1, :])]
        first = {rnd: min(u for u, t in enumerate(UNITS) if t["rnd"] == rnd) for rnd in range(6)}
        last = {rnd: max(u for u, t in enumerate(UNITS) if t["rnd"] == rnd) for rnd in range(6)}
        AHEAD = 3
        ORDER = []
        for u in range(len(UNITS) + AHEAD):
            wide = u < len(UNITS) and UNITS[u]["kind"] == "a"
            if wide:
                ORDER.append(("values", u - AHEAD))
            if u < len(UNITS):
                for rnd in range(6):
                    if first[rnd] == u:
                        ORDER += [("qk", n) for n, s in enumerate(SETS) if s[0] == rnd]
                ORDER.append(("scores", u))
            if u >= AHEAD and not wide:
                ORDER.append(("values", u - AHEAD))
        PIECES = [(c, part) for c in range(ADA_A, ADA) for part in range(4)]
        AT_ROUND = {0: 4, 1: 4, 2: 4, 3: 4, 4: 8, 5: 8}
        assert sum(AT_ROUND.values()) == len(PIECES)
        piece_buf = [m.oaT[:, :, :].rearrange("p a n -> p (a n)")[:, 0:2 * 512],
                     m.obT[:, :, :].rearrange("p a n -> p (a n)")[:, 256 + 512 + 512:256 + 512 + 512 + 2 * 512]]
        chunks_before = {rnd: sum(k for r, k in AT_ROUND.items() if r < rnd) // 4 for rnd in range(6)}
        ordered, ORDER = ORDER, []
        for what, n in ordered:
            ORDER.append((what, n))
            if what == "scores" and UNITS[n]["rnd"] in AT_ROUND:
                rnd = UNITS[n]["rnd"]
                k, x, size = AT_ROUND[rnd], n - first[rnd], last[rnd] - first[rnd] + 1
                ORDER += [("ada", 4 * chunks_before[rnd] + y) for y in range(k * x // size, k * (x + 1) // size)]
        OUT_T = [(c, m.obT, QB) for c in range(4)] + [(c, m.oaT, QA) for c in range(2)]

        mask_in, con_in, stored = sem("masks"), sem("tri"), sem("stored")
        own_t, own_d, own_a, zero = sem("own_rows_turned"), sem("own_rows_dve"), sem("own_rows_act"), sem("zeroed")
        cum, cum_out = sem("cum"), sem("cum_out")
        qk_t, qk_ao, qk_do = sem("qk_turned"), sem("qk_act_out"), sem("qk_dve_out")
        scores, seg_out, mx, ex = sem("scores"), sem("seg_out"), sem("max"), sem("exp")
        pt_t, pt_d, pt_a, pv, o_out, rd = sem("pt_turned"), sem("pt_dve"), sem("pt_act"), sem("pv"), sem("o_out"), sem("recip")
        piece_in = [sem("ada_in0"), sem("ada_in1")]
        ada, ada_out = sem("ada"), sem("ada_out")
        fin_t, fin_d, fin_a, dve_own = sem("out_turned"), sem("outT_dve"), sem("outT_act"), sem("dve_own")
        block = ctx.enter_context(nc.Block(no_gpsimd_drain=True))

        @block.sync
        def _(sp):
            sp.dma_start(tri, I["tri"]).then_inc(con_in, 16)
            sp.dma_start(masks[:], I["masks_prompt"]).then_inc(mask_in, 16)

            def piece(n):
                c, part = PIECES[n]
                if n >= 2:
                    sp.wait_ge(ada, n - 1)
                sp.dma_start(piece_buf[n % 2], I["w_ada"][c][:, part * 2 * 512:(part + 1) * 2 * 512]).then_inc(piece_in[n % 2], 16)
            piece(0)
            piece(1)
            n = 0
            for g in range(GROUPS):
                keep = min(WIN[g], SEQ) // P
                for part, col in ((0, KA), (1, VA)):
                    src = m.qkv[:, 4 - keep:4, col + g * AH * HD:col + (g + 1) * AH * HD]
                    dst = O[f"a{g + 1}_prompt"][:, part * AH * HD:(part + 1) * AH * HD].rearrange("(i p) n -> p i n", p=P)
                    sp.dma_start(dst, src).then_inc(stored, 16)
                    n += 1
                    for s in range(NSEQ):
                        sp.dma_start(O[f"a{g + 1}_sample"][s, BUFROWS[g] - DEC:BUFROWS[g], part * AH * HD:(part + 1) * AH * HD],
                                     m.qkv[s * DEC:(s + 1) * DEC, 4, col + g * AH * HD:col + (g + 1) * AH * HD]).then_inc(stored, 16)
                        n += 1
            for name, src in (("bk", m.qkv[:, :, KB:KB + BW]), ("bv", m.qkv[:, :, VB:VB + BW]), ("blogf", m.logf[:, :, :])):
                sp.dma_start(O[name + "_prompt"].rearrange("(i p) n -> p i n", p=P), src[:, 0:4, :]).then_inc(stored, 16)
                sp.dma_start(O[name + "_sample"], src[0:NS, 4, :]).then_inc(stored, 16)
                n += 2
            for x in range(2, len(PIECES)):
                piece(x)
            sp.wait_ge(stored, 16 * n)

        @block.gpsimd
        def _(pool):
            nc.gpsimd.memset(m.q_b[:], 0.0)
            nc.gpsimd.memset(m.q_a[:], 0.0).then_inc(zero, 1)

        @block.tensor
        def _(pe):
            def turn_probs(n, x):
                t = UNITS[n]
                g, (b, w) = t["grp0"] + x, t["groups"][x]
                if g >= 2:
                    pe.wait_ge(pt_a if g % 2 else pt_d, g // 2)
                for y in range(w):
                    mm = nc.tensor.transpose(m.banks[3 + g % 2][:, y * P:(y + 1) * P],
                                             sbuf[:, t["at"] + (b + y) * P:t["at"] + (b + y + 1) * P], m.ident[:, :])
                mm.then_inc(pt_t, 1)

            def weigh(n, x):
                t = UNITS[n]
                g, (b, w) = t["grp0"] + x, t["groups"][x]
                pe.wait_ge(pt_a if g % 2 else pt_d, g // 2 + 1)
                if x == 0 and n >= 2:
                    pe.wait_ge(o_out, n - 1)
                for y in range(w):
                    mm = nc.tensor.matmul(m.banks[5 + n % 2][:, 0:HD], pt[:, g % 3, y * P:(y + 1) * P], t["v"][b + y],
                                          start=b + y == 0, stop=b + y == len(t["v"]) - 1)
                mm.then_inc(pv, 1)

            for bank, cols in ((0, [QA + P * c for c in range(6)]), (1, [KA + P * c for c in range(6)]),
                               (2, [QB + P * c for c in range(4)] + [KB + P * c for c in range(4)])):
                for n, col in enumerate(cols):
                    mm = nc.tensor.transpose(m.banks[bank][:, n * NS:(n + 1) * NS], m.qkv[0:NS, 4, col:col + P], m.ident[0:NS, 0:NS])
                mm.then_inc(own_t, 1)
            pe.wait_ge(con_in, 16)
            for h in range(BH):
                if h >= 2:
                    pe.wait_ge(cum_out, h - 1)
                for j in range(4):
                    mm = nc.tensor.matmul(m.banks[3 + h % 2][:, j * P:SEQ], m.logf[:, j, h:h + 1].to_broadcast([P, P]),
                                          tri[:, 0:SEQ - j * P], start=j == 0, stop=j == 3)
                mm.then_inc(cum, 1)
            pe.wait_ge(own_d, 1)
            pe.wait_ge(own_a, 1)
            pe.wait_ge(cum_out, BH)
            for what, n in ORDER:
                if what == "qk":
                    rnd, col, _ = SETS[n]
                    if n >= 1:
                        pe.wait_ge(qk_ao if n % 2 else qk_do, (n + 1) // 2)
                    if chunks_before[rnd]:
                        pe.wait_ge(ada_out, chunks_before[rnd])
                    for i in range(4):
                        mm = nc.tensor.transpose(m.banks[7][:, i * P:(i + 1) * P], m.qkv[:, i, col:col + P], m.ident[:, :])
                    mm.then_inc(qk_t, 1)
                elif what == "ada":
                    c, part = PIECES[n]
                    pe.wait_ge(piece_in[n % 2], 16 * (n // 2 + 1))
                    if part == 0 and n:
                        pe.wait_ge(ada_out, n // 4)
                    r = 32 * (c % 4)
                    for k in range(2):
                        mm = nc.tensor.matmul(m.banks[7][r:r + 32, :], m.st[:, 2 * part + k, :], piece_buf[n % 2][:, 512 * k:512 * (k + 1)],
                                              start=part + k == 0, stop=part == 3 and k == 1)
                    mm.then_inc(ada, 1)
                elif what == "scores":
                    t = UNITS[n]
                    done = sum(1 for s in SETS if s[0] <= t["rnd"]) // 2
                    pe.wait_ge(qk_ao, done)
                    pe.wait_ge(qk_do, done)
                    for (bank, lhs, rhs, off, w), free in zip(t["segs"], t["bank_free"]):
                        if free:
                            pe.wait_ge(seg_out, free)
                        nc.tensor.matmul(m.banks[bank][:, 0:w], lhs, rhs, start=True, stop=True).then_inc(scores, 1)
                else:
                    t = UNITS[n]
                    pe.wait_ge(ex, n + 1)
                    for x in range(len(t["groups"])):
                        turn_probs(n, x)
                        if x or n:
                            weigh(*((n, x - 1) if x else (n - 1, len(UNITS[n - 1]["groups"]) - 1)))
            weigh(len(UNITS) - 1, len(UNITS[-1]["groups"]) - 1)
            pe.wait_ge(o_out, len(UNITS))
            for n, (c, dst, col) in enumerate(OUT_T):
                if n >= 2:
                    pe.wait_ge(fin_a if n % 2 else fin_d, n // 2)
                for i in range(4):
                    mm = nc.tensor.transpose(m.banks[n % 2][:, i * P:(i + 1) * P], m.qkv[:, i, col + c * P:col + (c + 1) * P], m.ident[:, :])
                mm.then_inc(fin_t, 1)

        @block.scalar
        def _(act):
            act.wait_ge(zero, 1)
            act.wait_ge(own_t, 1)
            for g in range(GROUPS):
                for h in range(AH):
                    r = 64 * (h % 2)
                    ins = nc.scalar.activation(m.q_a[r:r + 64, 2 * g + h // 2, :, DEC * h:DEC * (h + 1)],
                                               m.banks[0][r:r + 64, NS * (2 * g + h // 2):NS * (2 * g + h // 2 + 1)].rearrange("p (s q) -> p s q", q=DEC),
                                               ACT.Copy, scale=SCALE)
            ins.then_inc(own_a, 1)
            def result(n):
                t = UNITS[n]
                act.wait_ge(rd, n + 1)
                act.wait_ge(pv, t["grp0"] + len(t["groups"]))
                nc.scalar.activation(t["out"], m.banks[5 + n % 2][:, 0:HD], ACT.Copy, scale=den[:, 1, n:n + 1]).then_inc(o_out, 1)

            for what, n in ORDER:
                if what == "qk" and n % 2 == 0:
                    rnd, col, dst = SETS[n]
                    act.wait_ge(qk_t, n + 1)
                    if rnd == 4:
                        act.wait_ge(seg_out, UNITS[first[4]]["seg0"])
                    elif rnd >= 2:
                        w = UNITS[last[rnd - (1 if rnd == 5 else 2)]]
                        act.wait_ge(scores, w["seg0"] + len(w["segs"]))
                    nc.scalar.activation(dst, m.banks[7][:, :], ACT.Copy, scale=SCALE).then_inc(qk_ao, 1)
                elif what == "scores":
                    t = UNITS[n]
                    s = sbuf[:, t["at"]:t["at"] + t["width"]]
                    act.wait_ge(mx, n + 1)
                    nc.scalar.activation(s, s, ACT.Exp, bias=nmax[:, n:n + 1], accum_out=den[:, 0, n:n + 1]).then_inc(ex, 1)
                elif what == "values":
                    t = UNITS[n]
                    for x, (b, w) in enumerate(t["groups"]):
                        g = t["grp0"] + x
                        if g % 2:
                            act.wait_ge(pt_t, g + 1)
                            if g >= 3:
                                act.wait_ge(pv, g - 2)
                            nc.scalar.activation(pt[:, g % 3, 0:w * P], m.banks[3 + g % 2][:, 0:w * P], ACT.Copy).then_inc(pt_a, 1)
                    if n:
                        result(n - 1)
            result(len(UNITS) - 1)
            for n, (c, dst, col) in enumerate(OUT_T):
                if n % 2:
                    act.wait_ge(fin_t, n + 1)
                    nc.scalar.activation(dst[:, c, 0:SEQ], m.banks[n % 2][:, :], ACT.Copy).then_inc(fin_a, 1)
            act.wait_ge(fin_a, len(OUT_T) // 2)

        @block.vector
        def _(dve):
            own = Link(dve, dve_own)
            dve.wait_ge(zero, 1)
            dve.wait_ge(own_t, 3)
            for h in range(BH):
                r = 64 * (h % 2)
                nc.vector.tensor_scalar(m.q_b[r:r + 64, h // 2, :, DEC * h:DEC * (h + 1)],
                                        m.banks[2][r:r + 64, NS * (h // 2):NS * (h // 2 + 1)].rearrange("p (s q) -> p s q", q=DEC),
                                        SCALE, None, ALU.mult)
            nc.vector.tensor_copy(m.kn_b[:, :, :].rearrange("p a n -> p (a n)"), m.banks[2][:, 4 * NS:8 * NS])
            nc.vector.tensor_copy(m.kn_a[:, :, :].rearrange("p a n -> p (a n)"), m.banks[1][:, 0:6 * NS])
            nc.vector.tensor_copy(m.vn[:, 0:AW], m.qkv[0:NS, 4, VA:VA + AW])
            nc.vector.tensor_copy(m.vn[:, AW:AW + BW], m.qkv[0:NS, 4, VB:VB + BW])
            nc.vector.tensor_copy(m.lfn[:, :], m.logf[0:NS, 4, :]).then_inc(own_d, 1)
            for h in range(BH):
                dve.wait_ge(cum, h + 1)
                nc.vector.tensor_scalar(cb[:, h, :], m.banks[3 + h % 2][:, :], -1.0, None, ALU.mult).then_inc(cum_out, 1)
            dve.wait_ge(cum_out, BH)
            dve.wait_ge(mask_in, 16)
            diag = masks[:, P:2 * P]
            at_mask = (0, 256, 768)
            end_mask = (256, 768, 1280)
            for what, n in ORDER:
                if what == "qk" and n % 2 == 1:
                    rnd, col, dst = SETS[n]
                    dve.wait_ge(qk_t, n + 1)
                    if rnd == 4:
                        dve.wait_ge(seg_out, UNITS[first[4]]["seg0"])
                    elif rnd >= 2:
                        w = UNITS[last[rnd - (1 if rnd == 5 else 2)]]
                        dve.wait_ge(scores, w["seg0"] + len(w["segs"]))
                    nc.vector.tensor_copy(dst, m.banks[7][:, :]).then_inc(qk_do, 1)
                elif what == "ada" and PIECES[n][1] == 3:
                    c = PIECES[n][0]
                    dve.wait_ge(ada, n + 1)
                    mod = m.mod[32 * (c % 4):32 * (c % 4) + 32, c // 4, :]
                    nc.vector.tensor_tensor(mod, m.banks[7][32 * (c % 4):32 * (c % 4) + 32, :], mod, ALU.add).then_inc(ada_out, 1)
                elif what == "scores":
                    t = UNITS[n]
                    if t["buf_free"]:
                        dve.wait_ge(pt_t, t["buf_free"])
                    for x, (bank, lhs, rhs, off, w) in enumerate(t["segs"]):
                        dve.wait_ge(scores, t["seg0"] + x + 1)
                        s = sbuf[:, t["at"] + off:t["at"] + off + w]
                        bias = cb[:, t["h"], 0:w] if t["kind"] == "b" else masks[:, end_mask[x] - w:end_mask[x]]
                        nc.vector.tensor_tensor(s, m.banks[bank][:, 0:w], bias, ALU.add).then_inc(seg_out, 1)
                    dve.wait_ge(seg_out, t["seg0"] + len(t["segs"]))
                    if t["kind"] == "b":
                        s = sbuf[:, t["at"] + t["width"] - P:t["at"] + t["width"]]
                        own(nc.vector.tensor_tensor(s, s, diag, ALU.add))
                    nc.vector.tensor_reduce(nmax[:, n:n + 1], sbuf[:, t["at"]:t["at"] + t["width"]], AX, ALU.max, negate=True).then_inc(mx, 1)
                elif what == "values":
                    t = UNITS[n]
                    dve.wait_ge(ex, n + 1)
                    nc.vector.reciprocal(den[:, 1, n:n + 1], den[:, 0, n:n + 1]).then_inc(rd, 1)
                    for x, (b, w) in enumerate(t["groups"]):
                        g = t["grp0"] + x
                        if g % 2 == 0:
                            dve.wait_ge(pt_t, g + 1)
                            if g >= 3:
                                dve.wait_ge(pv, g - 2)
                            nc.vector.tensor_copy(pt[:, g % 3, 0:w * P], m.banks[3 + g % 2][:, 0:w * P]).then_inc(pt_d, 1)
            for n, (c, dst, col) in enumerate(OUT_T):
                if n % 2 == 0:
                    dve.wait_ge(fin_t, n + 1)
                    nc.vector.tensor_copy(dst[:, c, 0:SEQ], m.banks[n % 2][:, :]).then_inc(fin_d, 1)
            dve.wait_ge(ada_out, ADA - ADA_A)
            dve.wait_ge(fin_d, len(OUT_T) // 2)


def phase_c(nc, I, O, m):
    CK = 2
    NCH = PAGES // CK
    NB = BH * DEC
    NA = AH * DEC
    R = NB + NA
    W = PAST + GROUPS * DEC
    AT = 13
    A_CHUNKS = ((1, 0, 4), (2, 4, 4), (2, 8, 4), (0, 12, 1))
    A_COLS = AT * P
    with ExitStack() as ctx:
        sb = lambda name, shape, dt=F32: ctx.enter_context(nc.sbuf_tensor(name, shape, dt))
        sem = lambda name: ctx.enter_context(nc.semaphore("c_" + name))
        kr = sb("k_ring", [P, 4, CK, BW])
        vr = sb("v_ring", [P, 4, CK, BW])
        ak = sb("window_k", [P, AT, AH * HD])
        av = sb("window_v", [P, AT, AH * HD])
        kt = sb("k_t", [P, 2, 1024])
        bias = sb("bias", [R, PAST])
        sc = sb("score_rows", [R, W])
        pr = sb("prob_rows", [R, W])
        pt = sb("prob_t", [P, 19, R])
        qb = sb("q_b_now", [P, 4, NB])
        qa = sb("q_a_now", [P, 2 * GROUPS, NA])
        kb = sb("kn_b_now", [P, 4, DEC])
        ka = sb("kn_a_now", [P, 2 * GROUPS, DEC])
        vc = sb("v_now", [DEC, AW + BW])
        osb = sb("o_rows", [R, BW])
        own_mask = sb("head_mask", [R, BW])
        fold = sb("fold", [R, DEC])
        new_mask = sb("new_mask", [R, NS])
        new_bias = sb("new_bias", [NB, NS])
        nm = sb("neg_max", [R, 1])
        dn = sb("denom", [R, 2])
        pt_reg = sb("pages", [1, NSEQ * PAGES], I32)
        pt_col = sb("pages_col", [P, 1], I32)
        lf = vr[:, 0:1, :, :].rearrange("p a b n -> p (a b n)")
        cum = vr[:, 1:2, :, :].rearrange("p a b n -> p (a b n)").rearrange("p (h k) -> p h k", k=PAGE)
        ones = vr[:, 2, 0, 0:PAGE]
        pgt = vr[:, 2, 0, PAGE:2 * PAGE]
        seqof = vr[:, 2, 0, 2 * PAGE:2 * PAGE + NS]
        tri8 = vr[0:NS, 2, 0, 2 * PAGE + NS:2 * PAGE + 2 * NS]
        tot = vr[:, 2, 1, 0:BH]
        off = vr[:, 2, 1, BH:2 * BH]
        totx = vr[:, 2, 1, NB:2 * NB]
        lfx = vr[0:NS, 2, 1, 2 * NB:3 * NB]
        ccum = nc.dram_tensor("c_past", (NSEQ, BH, PAGES, PAGE), F32, kind="Internal").ap()
        vnew = nc.dram_tensor("v_new", (NS, AW + BW), F32, kind="Internal").ap()

        pages_in, pcol_in, con_in, lf_in, ccum_out, vnew_out = [sem(n) for n in ("pages", "pages_col", "const", "logf", "ccum", "vnew")]
        kin = [sem(f"k_in{b}") for b in range(4)]
        vin = [sem(f"v_in{b}") for b in range(4)]
        ak_in, av_in, vc_in, bias_in = sem("window_k"), sem("window_v"), sem("v_now"), sem("bias")
        turned, kt_d, kt_a, scored, new_scored, s_out = [sem(n) for n in ("turned", "t_dve", "t_act", "scored", "new_scored", "score_out")]
        cur, mx, ex, rd, v_used, pv_done, o_out = [sem(n) for n in ("now", "max", "exp", "recip", "v_used", "pv", "o_out")]
        scan, totals, pre, setup, dve_own, filled = [sem(n) for n in ("scan", "totals", "prefix", "setup", "dve_own", "filled")]
        block = ctx.enter_context(nc.Block(no_gpsimd_drain=True))
        PV_STEPS = 4
        STEPS = 12 + PV_STEPS
        CONSTS = 5

        def turns(eng, scores, values):
            scores(0, 0)
            with eng.Fori(1, NSEQ) as s:
                scores(s, s * STEPS - PV_STEPS)
                values(s - 1, s * STEPS - PV_STEPS + 12)
            values(NSEQ - 1, NSEQ * STEPS - PV_STEPS)

        def at_least(eng, s, value):
            if not isinstance(value, int) or value > 0:
                eng.wait_ge(s, value)

        row = lambda t, s, n: t[ds(s * n, n)]

        @block.sync
        def _(sp):
            ids = sorted(x.num for x in m.finished)
            assert ids == list(range(ids[0], ids[-1] + 1))
            sp.sem_clear(range(ids[0], ids[-1] + 1))
            sp.dma_start(pt_reg[:], I["page_table"]).then_inc(pages_in, 16)
            sp.dma_start(pt_col[:], I["page_table"].rearrange("a n -> n a")).then_inc(pcol_in, 16)
            sp.dma_start(vnew, m.vn[:]).then_inc(vnew_out, 16)
            sp.dma_start(bias[NB:R, 0:A_COLS], I["mask_window"]).then_inc(con_in, 16)
            sp.dma_start(own_mask[:], I["head_mask"]).then_inc(con_in, 16)
            sp.dma_start(fold[:], I["fold"]).then_inc(con_in, 16)
            sp.dma_start(new_mask[:], I["new_mask"]).then_inc(con_in, 16)
            sp.dma_start(vr[:, 2, 0, PAGE:2 * PAGE + 2 * NS], I["page_consts"]).then_inc(con_in, 16)
            sp.wait_ge(pages_in, 16)

            def pages(ring, source, arrived, s, ch):
                for y in range(CK):
                    v = sp.value_load(pt_reg[0:1, ds(s * PAGES + ch * CK + y, 1)], min_val=0, max_val=POOL - 1)
                    sp.dma_start(ring[:, ch % 4, y, :], source[ds(v, 1)].rearrange("a k n -> (a k) n")).then_inc(arrived[ch % 4], 16)

            def window(dst, arrived, s, part):
                c = slice(part * AH * HD, (part + 1) * AH * HD)
                sp.dma_start(dst[:, 0:4, :], I["cache_a2"][ds(s, 1), :, c].rearrange("a (p t) n -> p (a t) n", t=4)).then_inc(arrived, 16)
                sp.dma_start(dst[:, 4:12, :], I["cache_a3"][ds(s, 1), :, c].rearrange("a (p t) n -> p (a t) n", t=16)[:, 0:8, :]).then_inc(arrived, 16)
                sp.dma_start(dst[:, 12:13, :], I["cache_a1"][ds(s, 1), :, c].rearrange("a (p t) n -> p (a t) n", t=1)).then_inc(arrived, 16)

            def scores(s, base):
                for ch in range(NCH):
                    if ch >= 4:
                        sp.wait_ge(turned, base + 3 * ((ch - 4) // 2) + ch % 2 + 1)
                    elif not isinstance(s, int):
                        sp.wait_ge(scored, (s - 1) * 12 + 3 * ((ch + 4) // 2) + ch % 2 + 1)
                    pages(kr, I["cache_b_k"], kin, s, ch)
                    if ch == 3:
                        at_least(sp, scored, s * 12)
                        window(ak, ak_in, s, 0)
                        at_least(sp, s_out, s * 7)
                        if isinstance(s, int):
                            sp.wait_ge(ccum_out, 16 * NSEQ)
                        for h in range(BH):
                            sp.dma_start(bias[h * DEC:(h + 1) * DEC, :],
                                         ccum[ds(s, 1), h].rearrange("a g k -> a (g k)").to_broadcast([DEC, PAST])).then_inc(bias_in, 16)

            def values(v, base):
                at_least(sp, pv_done, v)
                window(av, av_in, v, 1)
                sp.dma_start(vc[:], vnew[ds(v * DEC, DEC), :]).then_inc(vc_in, 16)
                for ch in range(NCH):
                    at_least(sp, v_used, v * NCH + ch)
                    pages(vr, I["cache_b_v"], vin, v, ch)
            sp.sem_inc(v_used, 3)
            scores(0, 0)
            sp.wait_ge(vnew_out, 16)
            sp.wait_ge(setup, 1)
            with sp.Fori(1, NSEQ) as s:
                scores(s, s * STEPS - PV_STEPS)
                values(s - 1, None)
            values(NSEQ - 1, None)

        @block.gpsimd
        def _(pool):
            nc.gpsimd.memset(sc[:], NEG).then_inc(filled, 1)
            nc.gpsimd.memset(ones, 1.0).then_inc(filled, 1)
            pool.wait_ge(pcol_in, 16)
            pool.indirect_dma_start(out=lf, out_offset=None, in_=I["cache_b_logf"],
                                    in_offset=bass.IndirectOffsetOnAxis(ap=pt_col[:, 0:1], axis=0)).then_inc(lf_in, 16)

            def scores(s, base):
                at_least(pool, new_scored, s)
                one = lambda x: x[:, :, ds(s, 1), :].rearrange("p a b n -> p (a b) n")
                nc.gpsimd.tensor_copy(qb[:], one(m.q_b))
                nc.gpsimd.tensor_copy(qa[:], one(m.q_a))
                nc.gpsimd.tensor_copy(kb[:], m.kn_b[:, :, ds(s * DEC, DEC)])
                nc.gpsimd.tensor_copy(ka[:], m.kn_a[:, :, ds(s * DEC, DEC)]).then_inc(cur, 1)
            with pool.Fori(0, NSEQ) as s:
                scores(s, None)
            pool.wait_ge(cur, NSEQ)

        @block.tensor
        def _(pe):
            T = lambda n, x: m.banks[2 + 2 * (n % 2) + x]
            pe.wait_ge(con_in, 16 * CONSTS)
            pe.wait_ge(scan, BH + 1)
            nc.tensor.matmul(m.banks[6][:, 0:BH], pgt, tot, start=True, stop=True).then_inc(totals, 1)
            nc.tensor.matmul(m.banks[7][0:NB, 0:NS], lfx, tri8, start=True, stop=False)
            nc.tensor.matmul(m.banks[7][0:NB, 0:NS], totx, seqof, start=False, stop=True).then_inc(totals, 1)

            def turn_chunk(s, base, k):
                n = base + k
                c, x = k // 3, k % 3
                at_least(pe, kt_d, n - 1)
                at_least(pe, kt_a, n - 1)
                if x < 2:
                    ch = 2 * c + x
                    pe.wait_ge(kin[ch % 4], s * 64 + 32 * (ch // 4 + 1))
                    for pair in range(4):
                        for y in range(CK):
                            mm = nc.tensor.transpose(T(k, pair // 2)[:, (pair % 2) * 256 + y * P:(pair % 2) * 256 + (y + 1) * P],
                                                     kr[:, ch % 4, y, pair * P:(pair + 1) * P], m.ident[:, :])
                else:
                    g, t0, nt = A_CHUNKS[c]
                    pe.wait_ge(ak_in, s * 48 + 48)
                    for hp in range(2):
                        for y in range(nt):
                            mm = nc.tensor.transpose(T(k, hp)[:, y * P:(y + 1) * P], ak[:, t0 + y, hp * P:(hp + 1) * P], m.ident[:, :])
                mm.then_inc(turned, 1)

            def score_chunk(s, base, k):
                n = base + k
                c, x = k // 3, k % 3
                S = m.banks[c % 2]
                if x == 0:
                    at_least(pe, s_out, s * 7 + (c - 1 if c >= 2 else 0))
                pe.wait_ge(kt_d, n + 1)
                pe.wait_ge(kt_a, n + 1)
                if x < 2:
                    for pair in range(4):
                        mm = nc.tensor.matmul(S[0:NB, x * 256:(x + 1) * 256], qb[:, pair, :], kt[:, k % 2, pair * 256:(pair + 1) * 256],
                                              start=pair == 0, stop=pair == 3)
                else:
                    g, t0, nt = A_CHUNKS[c]
                    for hp in range(2):
                        mm = nc.tensor.matmul(S[NB:R, 0:nt * P], qa[:, 2 * g + hp, :], kt[:, k % 2, hp * 512:hp * 512 + nt * P],
                                              start=hp == 0, stop=hp == 1)
                mm.then_inc(scored, 1)

            def scores(s, base):
                pe.wait_ge(cur, s + 1)
                turn_chunk(s, base, 0)
                for k in range(12):
                    if k < 11:
                        turn_chunk(s, base, k + 1)
                    score_chunk(s, base, k)
                pe.wait_ge(s_out, s * 7 + 3)
                for pair in range(4):
                    nc.tensor.matmul(m.banks[0][0:NB, 0:DEC], qb[:, pair, :], kb[:, pair, :], start=pair == 0, stop=pair == 3)
                for g in range(GROUPS):
                    for hp in range(2):
                        mm = nc.tensor.matmul(m.banks[0][NB:R, g * DEC:(g + 1) * DEC], qa[:, 2 * g + hp, :], ka[:, 2 * g + hp, :],
                                              start=hp == 0, stop=hp == 1)
                mm.then_inc(new_scored, 1)

            def values(v, base):
                pe.wait_ge(ex, v + 1)
                for j in range(2):
                    pe.wait_ge(kt_d, base + j - 1)
                    pe.wait_ge(kt_a, base + j - 1)
                    for b in range(10 * j, min(10 * j + 10, 19)):
                        w = P if b < PAGES else DEC
                        c = b * P if b < PAGES else PAST + (b - PAGES) * DEC
                        mm = nc.tensor.transpose(T(j, b % 10 // 5)[0:w, (b % 5) * R:(b % 5 + 1) * R], pr[:, c:c + w], m.ident[0:R, 0:R])
                    mm.then_inc(turned, 1)
                at_least(pe, o_out, v * 2)
                for ch in range(NCH):
                    if ch * CK % 10 == 0:
                        pe.wait_ge(kt_d, base + ch * CK // 10 + 1)
                        pe.wait_ge(kt_a, base + ch * CK // 10 + 1)
                    pe.wait_ge(vin[ch % 4], v * 64 + 32 * (ch // 4 + 1))
                    for y in range(CK):
                        mm = nc.tensor.matmul(m.banks[6][0:NB, :], pt[:, ch * CK + y, 0:NB], vr[:, ch % 4, y, :],
                                              start=ch + y == 0, stop=False)
                    mm.then_inc(v_used, 1)
                pe.wait_ge(vc_in, v * 16 + 16)
                nc.tensor.matmul(m.banks[6][0:NB, :], pt[0:DEC, PAGES, 0:NB], vc[:, AW:AW + BW], start=False, stop=True)
                pe.wait_ge(av_in, v * 48 + 48)
                for b in range(AT):
                    nc.tensor.matmul(m.banks[6][NB:R, 0:256], pt[:, b, NB:R], av[:, b, :], start=b == 0, stop=False)
                for g in range(GROUPS):
                    mm = nc.tensor.matmul(m.banks[6][NB:R, 0:256], pt[0:DEC, PAGES + g, NB:R], vc[:, g * 256:(g + 1) * 256],
                                          start=False, stop=g == GROUPS - 1)
                mm.then_inc(pv_done, 1)
                pe.wait_ge(o_out, v * 2 + 2)
                for j in range(2, 4):
                    pe.wait_ge(kt_d, base + j - 1)
                    pe.wait_ge(kt_a, base + j - 1)
                    if j == 2:
                        for pair in range(4):
                            mm = nc.tensor.matmul(T(j, pair // 2)[:, (pair % 2) * DEC:(pair % 2 + 1) * DEC],
                                                  osb[0:NB, pair * P:(pair + 1) * P], fold[0:NB, :], start=True, stop=True)
                    else:
                        for hp in range(2):
                            mm = nc.tensor.matmul(T(j, hp)[:, 0:DEC], osb[NB:R, hp * P:(hp + 1) * P], fold[NB:R, :], start=True, stop=True)
                    mm.then_inc(turned, 1)
            turns(pe, scores, values)

        def copy_keys(eng, copy, out_sem, x, s, base, k):
            n = base + k
            eng.wait_ge(turned, n + 1)
            at_least(eng, scored, s * 12 + k - 1)
            c = k // 3
            w = 512 if k % 3 < 2 else A_CHUNKS[c][2] * P
            copy(kt[:, k % 2, x * 512:x * 512 + w], m.banks[2 + 2 * (k % 2) + x][:, 0:w]).then_inc(out_sem, 1)

        def copy_probs(eng, copy, out_sem, x, v, base, j):
            eng.wait_ge(turned, base + j + 1)
            at_least(eng, pv_done, v)
            T = m.banks[2 + 2 * (j % 2) + x][:, 0:5 * R].rearrange("p (b r) -> p b r", r=R)
            b0 = 10 * j + 5 * x
            if b0 < 15:
                copy(pt[:, b0:b0 + 5, :], T).then_inc(out_sem, 1)
            else:
                copy(pt[:, 15, :], T[:, 0, :])
                copy(pt[0:DEC, 16:19, :], T[0:DEC, 1:4, :]).then_inc(out_sem, 1)

        def copy_outs(eng, copy, out_sem, x, v, base, j):
            eng.wait_ge(turned, base + j + 1)
            T = m.banks[2 + 2 * (j % 2) + x]
            cols = ds(v * DEC + SEQ, DEC)
            if j == 2:
                copy(m.obT[:, 2 * x:2 * x + 2, cols], T[:, 0:2 * DEC].rearrange("p (a q) -> p a q", q=DEC)).then_inc(out_sem, 1)
            else:
                copy(m.oaT[:, x, cols], T[:, 0:DEC]).then_inc(out_sem, 1)

        @block.scalar
        def _(act):
            for s in range(NSEQ):
                if s == 0:
                    act.wait_ge(pre, BH + 1)
                act.dma_start(ccum[s].rearrange("h g k -> g h k"), cum[s * PAGES:(s + 1) * PAGES, :, :]).then_inc(ccum_out, 16)
            act.wait_ge(ccum_out, 16 * NSEQ)
            act.sem_inc(setup, 1)
            copy = lambda o, i: nc.scalar.activation(o, i, ACT.Copy)

            def scores(s, base):
                for k in range(12):
                    copy_keys(act, copy, kt_a, 1, s, base, k)
                if isinstance(s, int):
                    soften(s)

            def soften(s):
                act.wait_ge(mx, s + 1)
                at_least(act, rd, s)
                nc.scalar.activation(pr[:], sc[:], ACT.Exp, bias=nm[:, 0:1], accum_out=dn[:, 0:1]).then_inc(ex, 1)

            def values(v, base):
                for j in range(2):
                    copy_probs(act, copy, kt_a, 1, v, base, j)
                for j in range(2, 4):
                    copy_outs(act, copy, kt_a, 1, v, base, j)
                if not isinstance(v, int):
                    act.wait_ge(turned, base + 2)
                    soften(v + 1)
            turns(act, scores, values)
            act.wait_ge(kt_a, NSEQ * STEPS)

        @block.vector
        def _(dve):
            own = Link(dve, dve_own)
            copy = lambda o, i: nc.vector.tensor_copy(o, i)
            dve.wait_ge(lf_in, 16)
            dve.wait_ge(filled, 2)
            by_head = lf.rearrange("p (k h) -> p h k", h=BH)
            for h in range(BH):
                nc.vector.tensor_tensor_scan(cum[:, h, :], ones, by_head[:, h, :], 0.0, ALU.mult, ALU.add).then_inc(scan, 1)
            dve.wait_ge(scan, BH)
            dve.wait_ge(con_in, 16 * CONSTS)
            last_key = cum[:, :, PAGE - 1:PAGE]
            nc.vector.tensor_copy(tot, last_key.rearrange("p h a -> p (h a)"))
            nc.vector.tensor_copy(totx.rearrange("p (h q) -> p h q", q=DEC), last_key.to_broadcast([P, BH, DEC]))
            nc.vector.tensor_copy(lfx.rearrange("p (h q) -> p h q", q=DEC),
                                  m.lfn[:, :].unsqueeze(2).to_broadcast([NS, BH, DEC])).then_inc(scan, 1)
            dve.wait_ge(totals, 2)
            own(nc.vector.tensor_copy(off, m.banks[6][:, 0:BH]))
            for h in range(BH):
                nc.vector.tensor_scalar(cum[:, h, :], cum[:, h, :], off[:, h:h + 1], -1.0, ALU.add, ALU.mult).then_inc(pre, 1)
            nc.vector.scalar_tensor_tensor(new_bias[:], m.banks[7][0:NB, 0:NS], -1.0, new_mask[0:NB, :], ALU.mult, ALU.add).then_inc(pre, 1)
            dve.wait_ge(pre, BH + 1)

            def scores(s, base):
                for k in range(12):
                    copy_keys(dve, copy, kt_d, 0, s, base, k)
                    if k % 3 == 0 and k > 0:
                        add_bias(s, k // 3 - 1)
                add_bias(s, 3)
                dve.wait_ge(new_scored, s + 1)
                nc.vector.tensor_tensor(sc[0:NB, PAST:PAST + DEC], m.banks[0][0:NB, 0:DEC],
                                        new_bias[:, ds(s * DEC, DEC)], ALU.add).then_inc(s_out, 1)
                nc.vector.tensor_tensor(sc[NB:R, PAST:W], m.banks[0][NB:R, 0:GROUPS * DEC], new_mask[NB:R, 0:GROUPS * DEC],
                                        ALU.add).then_inc(s_out, 1)
                dve.wait_ge(s_out, s * 7 + 7)
                nc.vector.tensor_reduce(nm[:, 0:1], sc[:], AX, ALU.max, negate=True).then_inc(mx, 1)

            def add_bias(s, c):
                dve.wait_ge(scored, s * 12 + 3 * c + 3)
                if c == 0:
                    at_least(dve, ex, s)
                    dve.wait_ge(bias_in, s * 16 * BH + 16 * BH)
                S = m.banks[c % 2]
                cols = slice(512 * c, 512 * (c + 1))
                if c < 3:
                    nc.vector.tensor_tensor(sc[:, cols], S[0:R, :], bias[:, cols], ALU.add).then_inc(s_out, 1)
                else:
                    nc.vector.tensor_tensor(sc[0:NB, cols], S[0:NB, :], bias[0:NB, cols], ALU.add).then_inc(s_out, 1)
                    nc.vector.tensor_tensor(sc[NB:R, 512 * c:A_COLS], S[NB:R, 0:P], bias[NB:R, 512 * c:A_COLS], ALU.add).then_inc(s_out, 1)

            def values(v, base):
                dve.wait_ge(ex, v + 1)
                at_least(dve, o_out, v * 2)
                nc.vector.reciprocal(dn[:, 1:2], dn[:, 0:1]).then_inc(rd, 1)
                for j in range(2):
                    copy_probs(dve, copy, kt_d, 0, v, base, j)
                dve.wait_ge(pv_done, v + 1)
                dve.wait_ge(rd, v + 1)
                at_least(dve, turned, base)
                for rows, w in ((slice(0, NB), BW), (slice(NB, R), AH * HD)):
                    nc.vector.scalar_tensor_tensor(osb[rows, 0:w], m.banks[6][rows, 0:w], dn[rows, 1:2], own_mask[rows, 0:w],
                                                   ALU.mult, ALU.mult).then_inc(o_out, 1)
                for j in range(2, 4):
                    copy_outs(dve, copy, kt_d, 0, v, base, j)
            turns(dve, scores, values)
            dve.wait_ge(kt_d, NSEQ * STEPS)


def phase_d(nc, I, O, m):
    with ExitStack() as ctx:
        sb = lambda name, shape, dt=F32: ctx.enter_context(nc.sbuf_tensor(name, shape, dt))
        sem = lambda name: ctx.enter_context(nc.semaphore("d_" + name))
        LW = NG + EXPERTS
        PLACES = (0, 4 * KD * 512, 4 * KD * 512 + 2 * D, 4 * KD * 512 + 6 * D, 4 * KD * 512 + 8 * D)
        assert PLACES[-1] <= RING * EXPERT_W
        wg, wpa, wpb, sg = (m.w[:, lo:hi] for lo, hi in zip(PLACES[:-1], PLACES[1:]))
        wg = wg.rearrange("p (a n) -> p a n", a=4)
        wo = wg[:, 0:2, :].rearrange("p a n -> p (a n)").rearrange("p (k n) -> p k n", n=D)
        wpa = wpa.rearrange("p (a n) -> p a n", a=2)
        wpb = wpb.rearrange("p (a n) -> p a n", a=4)
        mix = sb("mix", [P, TILES, D])
        gains = (mix[:, 0, :], mix[:, 1, :])
        sg = sg.rearrange("p (u b n) -> p u b n", u=2, b=2)
        junk = sb("squares", [P, D])
        wr = sb("w_router", [P, KD, LW])
        br = sb("b_router", [P, LW])
        ss = sb("sums", [P, TILES, 8])
        lg = sb("logits", [P, TILES, LW])
        g8 = sb("group8", [P, TILES, 8])
        gm = sb("group_max", [P, TILES, 8])
        gi = sb("group_index", [P, TILES, 8], U32)
        le = sb("expert_logits", [P, TILES, 8])
        lm = sb("expert_max", [P, TILES, 8])
        li = sb("expert_index", [P, TILES, 8], U32)
        iota = sb("iota", [P, EXPERTS])
        tok = sb("row_ids", [P, TILES], I32)
        valid = sb("valid", [P, TILES])
        ohg = sb("group_onehot", [P, TILES, NG])
        t32 = m.mod[:, 0, 2 * P:2 * P + TILES * EXPERTS].rearrange("p (i e) -> p i e", e=EXPERTS)
        oh = junk[:, 0:3 * TILES * EXPERTS].rearrange("p (c i e) -> p c i e", c=3, i=TILES)
        f = sb("per_row", [P, 16, TILES])
        cnt = sb("counts", [P, 4, EXPERTS])
        rankc = m.mod[:, 0, 0:2 * P]
        OWN = OVER // 2
        own32 = junk[0:1, 3 * TILES * EXPERTS:3 * TILES * EXPERTS + OWN * EXPERTS].rearrange("p (j e) -> p j e", e=EXPERTS)
        zero = sb("zeros", [SLOTS, BLOCKS], I32)
        post = sb("table_at", [P, TILES, TOPK], I32)
        later = sb("over_ids", [1, OVER])
        chunk_in = [sem(f"gates{n}") for n in range(4)]
        rank_in = sem("rank_consts")
        gain_in, pa_in, wo_in, x_in, con_in, zeroed, table_z, h2_out = [sem(n) for n in (
            "gains", "w_p", "w_o", "rows", "const", "zeros", "table_zero", "h2_out")]
        spread, spread_out, m_pe, m_act, m_y, m_dve = [sem(n) for n in ("spread", "spread_out", "merge", "sigmoid", "weighted", "mixed")]
        t_pe, t_d, t_a, wo_pe, wo_out, sq, rq, rs = [sem(n) for n in ("turned", "t_dve", "t_act", "w_o_out", "w_o_read", "squares", "mean", "rstd")]
        x_ok, hn, h_ok, lg_pe, lg_out = [sem(n) for n in ("residual", "scaled", "h2", "logits", "logits_out")]
        dve_own, act_own, ex_in, ex_out, oh_ok, rank_pe, pos_ok, placed = [sem(n) for n in (
            "dve_own", "act_own", "exp_in", "exp_out", "onehots", "ranks", "positions", "placed")]
        block = ctx.enter_context(nc.Block(no_gpsimd_drain=True))
        spread_pe, spread_dve, SPREAD = spread_steps(m, [(2, 4, gains[0]), (0, 8, gains[1]), (1, 6, None)], spread, spread_out)
        ORDER = [("merge", 0, i) for i in range(TILES)]
        for i in range(TILES + 2):
            if i < TILES:
                ORDER.append(("merge", 1, i))
            if 1 <= i <= TILES:
                ORDER.append(("mix", 0, i - 1))
            if i == TILES:
                ORDER.append(("norm", 0, i - 2))
            if i >= 2:
                ORDER.append(("route", 0, i - 2))
            if 1 <= i <= TILES and i != TILES - 1:
                ORDER.append(("norm", 0, i - 1))
        mix_bank = lambda i, h: m.banks[(6 if i < TILES - 1 else 2) + h]

        def filled(i):
            return (slice(0, P), 512) if len(parts(i, 512)) == 1 else (slice(0, 2 * ROWS[i]), 256)

        @block.sync
        def _(sp):
            sp.dma_start(gains[0], I["g_post_mix"].partition_broadcast(P)).then_inc(gain_in, 16)
            sp.dma_start(gains[1], I["g_pre_ffn"].partition_broadcast(P)).then_inc(gain_in, 16)
            for n in (0, 2):
                sp.dma_start(wg[:, n // 2, :], I["w_gates"][n]).then_inc(chunk_in[n // 2], 16)
            sp.dma_start(m.w[:, PLACES[1]:PLACES[2]], I["w_pa"]).then_inc(pa_in, 16)
            sp.dma_start(m.w[:, PLACES[2]:PLACES[3]], I["w_pb"]).then_inc(pa_in, 16)
            for n in (1, 3):
                sp.dma_start(wg[:, 2 + n // 2, :], I["w_gates"][n]).then_inc(chunk_in[2 + n // 2], 16)
            for i in range(TILES):
                src = I["x_prompt"][i * P:(i + 1) * P, :] if i < TILES - 1 else I["x_sample"]
                sp.dma_start(m.x1[0:ROWS[i], i, :], src).then_inc(x_in, 16)
            for dst, name in ((iota, "iota"), (tok, "row_ids"), (valid, "valid")):
                sp.dma_start(dst[:], I[name]).then_inc(con_in, 16)
            sp.dma_start(wr[:].rearrange("p a n -> p (a n)"), I["w_r"]).then_inc(con_in, 16)
            sp.dma_start(br[:], I["b_r"].partition_broadcast(P)).then_inc(con_in, 16)
            sp.dma_start(later[:], I["over_ids"]).then_inc(con_in, 16)
            sp.dma_start(rankc, I["rank_consts"]).then_inc(rank_in, 16)
            sp.wait_ge(zeroed, 1)
            sp.dma_start(m.table, zero[:]).then_inc(table_z, 16)
            sp.wait_ge(m_pe, 4 * TILES)
            sp.dma_start(wo.rearrange("p k n -> p (k n)"), I["w_o"]).then_inc(wo_in, 16)

            def rows_out(i):
                sp.wait_ge(h_ok, i + 1)
                sp.dma_start(m.h2[i * P:i * P + ROWS[i], :], mix[0:ROWS[i], i, :]).then_inc(h2_out, 16)

            def expert_in(u):
                sp.dma_start(m.weights(u), I["w_exp"][u]).then_inc(m.w_in[u], 16)
            sp.wait_ge(m_pe, 8 * TILES)
            sp.wait_ge(m_dve, 2 * TILES)
            expert_in(0)
            expert_in(1)
            for i in range(TILES - 2):
                rows_out(i)
            sp.wait_ge(wo_pe, 2 * TILES)
            expert_in(2)
            expert_in(3)
            rows_out(TILES - 2)
            rows_out(TILES - 1)
            sp.wait_ge(h2_out, 16 * TILES)

        @block.tensor
        def _(pe):
            spread_pe(nc, pe)
            pe.wait_ge(spread_out, SPREAD)
            units = turns = routes = 0
            for what, half, i in ORDER:
                r = slice(i * P, i * P + ROWS[i])
                if what == "merge":
                    u = units
                    units += 1
                    for b in range(2):
                        if u:
                            pe.wait_ge(m_act, 2 * u - 1 + b)
                        pe.wait_ge(chunk_in[2 * half + b], 16)
                        for k in range(KD):
                            for lo, hi, at in parts(i, 512):
                                mm = nc.tensor.matmul(m.banks[b][at:at + ROWS[i], 0:hi - lo], m.hT[:, k, r],
                                                      wg[:, 2 * half + b, 512 * k + lo:512 * k + hi], start=k == 0, stop=k == KD - 1)
                        mm.then_inc(m_pe, 1)
                    for b, o, w, nk in ((2, m.oaT, wpa, 2), (3, m.obT, wpb, 4)):
                        if u:
                            pe.wait_ge(m_y, 2 * u - 3 + b)
                        pe.wait_ge(pa_in, 32)
                        for k in range(nk):
                            for lo, hi, at in parts(i, 512):
                                mm = nc.tensor.matmul(m.banks[b][at:at + ROWS[i], 0:hi - lo], o[:, k, r],
                                                      w[:, k, half * 512 + lo:half * 512 + hi], start=k == 0, stop=k == nk - 1)
                        mm.then_inc(m_pe, 1)
                    continue
                if what == "norm":
                    continue
                t = turns
                turns += 1
                pe.wait_ge(t_d, t)
                pe.wait_ge(t_a, t)
                if routes:
                    pe.wait_ge(lg_out, routes)
                if what == "mix":
                    pe.wait_ge(m_dve, TILES + i + 1)
                else:
                    pe.wait_ge(h_ok, i + 1)
                for k in range(KD):
                    mm = nc.tensor.transpose(m.banks[4 + k // 4][:, (k % 4) * P:(k % 4) * P + ROWS[i]],
                                             mix[0:ROWS[i], i, k * P:(k + 1) * P], m.ident[0:ROWS[i], 0:ROWS[i]])
                mm.then_inc(t_pe, 1)
                pe.wait_ge(t_d, t + 1)
                pe.wait_ge(t_a, t + 1)
                if what == "mix":
                    pe.wait_ge(wo_in, 16)
                    for h in range(2):
                        if i == TILES - 1:
                            pe.wait_ge(m_y, 4 * TILES)
                        elif i:
                            pe.wait_ge(wo_out, 2 * i - 1 + h)
                        for k in range(KD):
                            mm = nc.tensor.matmul(mix_bank(i, h)[0:ROWS[i], :], m.hT[:, k, r], wo[:, k, h * 512:h * 512 + 512],
                                                  start=k == 0, stop=k == KD - 1)
                        mm.then_inc(wo_pe, 1)
                else:
                    pe.wait_ge(con_in, 16 * 6)
                    for k in range(KD):
                        mm = nc.tensor.matmul(m.banks[4][0:ROWS[i], 0:LW], m.hT[:, k, r], wr[:, k, :], start=k == 0, stop=k == KD - 1)
                    mm.then_inc(lg_pe, 1)
                    routes += 1
            pe.wait_ge(oh_ok, 1)
            pe.wait_ge(rank_in, 16)
            pe.wait_ge(lg_out, TILES)
            strict, ones = rankc[:, 0:P], rankc[:, P:2 * P]
            for i in range(TILES + 1):
                out = m.banks[0][:, i * EXPERTS:(i + 1) * EXPERTS] if i < TILES else m.banks[1][:, 0:EXPERTS]
                upto = min(i + 1, TILES)
                for j in range(upto):
                    mm = nc.tensor.matmul(out, strict if j == i else ones, oh[:, 2, j, :], start=j == 0, stop=j == upto - 1)
            mm.then_inc(rank_pe, 1)

        @block.scalar
        def _(act):
            own = Link(act, act_own)
            units = turns = 0
            for what, half, i in ORDER:
                rows = slice(0, ROWS[i])
                if what == "merge":
                    u = units
                    units += 1
                    for b in range(2):
                        act.wait_ge(m_pe, 4 * u + 1 + b)
                        if u >= 2:
                            act.wait_ge(m_dve, u - 1)
                        rows, width = filled(i)
                        nc.scalar.activation(sg[rows, u % 2, b, 0:width], m.banks[b][rows, 0:width], ACT.Exp, scale=-1.0).then_inc(m_act, 1)
                    continue
                if what != "norm":
                    turns += 1
                    act.wait_ge(t_pe, turns)
                    nc.scalar.activation(m.hT[:, 4:8, i * P:i * P + ROWS[i]],
                                         m.banks[5][:, :].rearrange("p (k r) -> p k r", r=P)[:, :, 0:ROWS[i]], ACT.Copy).then_inc(t_a, 1)
                    continue
                for h in range(2):
                    act.wait_ge(wo_pe, 2 * i + 1 + h)
                    own(nc.scalar.activation(junk[rows, 0:512], mix_bank(i, h)[rows, :], ACT.Square, accum_out=ss[rows, i, h:h + 1]))
                act.sem_inc(sq, 1)
                for y in range(2):
                    if y:
                        act.wait_ge(x_ok, i + 1)
                        own(nc.scalar.activation(junk[rows, :], m.x1[rows, i, :], ACT.Square, accum_out=ss[rows, i, 2:3]))
                        act.sem_inc(sq, 1)
                    act.wait_ge(rq, 2 * i + y + 1)
                    own(nc.scalar.activation(ss[rows, i, 4 + y:5 + y], ss[rows, i, 3:4], ACT.Ln))
                    nc.scalar.activation(ss[rows, i, 6 + y:7 + y], ss[rows, i, 4 + y:5 + y], ACT.Exp, scale=-0.5).then_inc(rs, 1)
            act.wait_ge(ex_in, 1)
            nc.scalar.activation(ohg[:], ohg[:], ACT.Exp).then_inc(ex_out, 1)
            act.wait_ge(ex_in, 2)
            nc.scalar.activation(f[:, 1, :], f[:, 0, :], ACT.Exp).then_inc(ex_out, 1)
            act.wait_ge(ex_out, 2)

        @block.gpsimd
        def _(pool):
            nc.gpsimd.memset(zero[:], 0)
            nc.gpsimd.memset(lg[:], 0.0)
            nc.gpsimd.memset(g8[:], NEG).then_inc(zeroed, 1)
            for i in range(TILES):
                rows = slice(0, ROWS[i])
                pool.wait_ge(hn, i + 1)
                nc.gpsimd.tensor_tensor(mix[rows, i, :], mix[rows, i, :], scale_of(m, i, 1)[rows], ALU.add).then_inc(h_ok, 1)
            pool.wait_ge(h_ok, TILES)
            pool.wait_ge(table_z, 16)
            pool.wait_ge(con_in, 16 * 6)
            for c in range(TOPK):
                pool.wait_ge(pos_ok, c + 1)
                for i in range(TILES):
                    pool.indirect_dma_start(out=m.table.rearrange("a (b c) -> (a b) c", c=1),
                                            out_offset=bass.IndirectOffsetOnAxis(ap=post[0:ROWS[i], i, c:c + 1], axis=0),
                                            in_=tok[0:ROWS[i], i:i + 1], in_offset=None).then_inc(placed, 16)
            pool.wait_ge(placed, 16 * TILES * TOPK)

        @block.vector
        def _(dve):
            own = Link(dve, dve_own)
            dve.wait_ge(gain_in, 32)
            spread_dve(nc, dve)
            dve.wait_ge(spread_out, SPREAD)
            dve.wait_ge(x_in, 16 * TILES)
            dve.wait_ge(con_in, 16 * 6)
            dve.wait_ge(zeroed, 1)
            units = turns = 0
            for what, half, i in ORDER:
                rows = slice(0, ROWS[i])
                if what == "merge":
                    u = units
                    units += 1
                    for b in range(2):
                        rows, width = filled(i)
                        s = sg[rows, u % 2, b, 0:width]
                        dve.wait_ge(m_act, 2 * u + 1 + b)
                        own(nc.vector.tensor_scalar(s, s, 1.0, None, ALU.add))
                        own(nc.vector.reciprocal(s, s))
                        dve.wait_ge(m_pe, 4 * u + 3 + b)
                        nc.vector.tensor_tensor(s, m.banks[2 + b][rows, 0:width], s, ALU.mult).then_inc(m_y, 1)
                    dve.wait_ge(m_y, 2 * u + 2)
                    for lo, hi, at in parts(i, 512):
                        a, b = (sg[at:at + ROWS[i], u % 2, x, 0:hi - lo] for x in range(2))
                        ins = nc.vector.tensor_tensor(mix[0:ROWS[i], i, half * 512 + lo:half * 512 + hi], a, b, ALU.add)
                    ins.then_inc(m_dve, 1)
                    continue
                if what != "norm":
                    turns += 1
                    dve.wait_ge(t_pe, turns)
                    nc.vector.tensor_copy(m.hT[:, 0:4, i * P:i * P + ROWS[i]],
                                          m.banks[4][:, :].rearrange("p (k r) -> p k r", r=P)[:, :, 0:ROWS[i]]).then_inc(t_d, 1)
                    if what == "route":
                        dve.wait_ge(lg_pe, i + 1)
                        nc.vector.tensor_tensor(lg[rows, i, :], m.banks[4][rows, 0:LW], br[rows, :], ALU.add).then_inc(lg_out, 1)
                    continue
                dve.wait_ge(sq, 2 * i + 1)
                own(nc.vector.tensor_tensor(ss[rows, i, 0:1], ss[rows, i, 0:1], ss[rows, i, 1:2], ALU.add))
                nc.vector.tensor_scalar(ss[rows, i, 3:4], ss[rows, i, 0:1], 1.0 / D, EPS, ALU.mult, ALU.add).then_inc(rq, 1)
                dve.wait_ge(rs, 2 * i + 1)
                for h in range(2):
                    c = slice(h * 512, h * 512 + 512)
                    nc.vector.scalar_tensor_tensor(mix[rows, i, c], mix_bank(i, h)[rows, :], ss[rows, i, 6:7],
                                                   scale_of(m, i, 2)[rows, c], ALU.mult, ALU.mult).then_inc(wo_out, 1)
                dve.wait_ge(wo_out, 2 * i + 2)
                nc.vector.tensor_tensor(m.x1[rows, i, :], m.x1[rows, i, :], mix[rows, i, :], ALU.add).then_inc(x_ok, 1)
                dve.wait_ge(x_ok, i + 1)
                dve.wait_ge(sq, 2 * i + 2)
                nc.vector.tensor_scalar(ss[rows, i, 3:4], ss[rows, i, 2:3], 1.0 / D, EPS, ALU.mult, ALU.add).then_inc(rq, 1)
                dve.wait_ge(rs, 2 * i + 2)
                nc.vector.scalar_tensor_tensor(mix[rows, i, :], m.x1[rows, i, :], ss[rows, i, 7:8], scale_of(m, i, 0)[rows],
                                               ALU.mult, ALU.mult).then_inc(hn, 1)
            V = nc.vector
            MORE = -(-NT // SLOTS) - 1
            used = 3 * TILES * EXPERTS + EXPERTS * MORE
            past = junk[:, used:used + TILES * MORE].rearrange("p (i k) -> p i k", k=MORE)
            steps = junk[:, used + TILES * MORE:used + TILES * MORE + MORE]
            dve.wait_ge(sq, 2 * TILES)
            own(V.tensor_scalar(steps, iota[:, 1:1 + MORE], float(SLOTS), None, ALU.mult))
            dve.wait_ge(lg_out, TILES)
            own(V.tensor_copy(g8[:, :, 0:NG], lg[:, :, 0:NG]))
            for i in range(TILES):
                ins = V.max(gm[:, i, :], g8[:, i, :])
            own(ins)
            for i in range(TILES):
                ins = V.max_index(gi[:, i, :], gm[:, i, :], g8[:, i, :])
            own(ins)
            own(V.tensor_tensor(ohg[:], lg[:, :, 0:NG], gm[:, :, 0:1].to_broadcast([P, TILES, NG]), ALU.subtract))
            dve.sem_inc(ex_in, 1)
            dve.wait_ge(ex_out, 1)
            own(V.tensor_reduce(f[:, 2, :], ohg[:], AX, ALU.add))
            own(V.reciprocal(f[:, 2, :], f[:, 2, :]))
            own(V.tensor_copy(f[:, 3, :], gi[:, :, 0:1].rearrange("p i a -> p (i a)")))
            own(V.tensor_tensor(ohg[:], iota[:, 0:NG].unsqueeze(1).to_broadcast([P, TILES, NG]),
                                f[:, 3, :].unsqueeze(2).to_broadcast([P, TILES, NG]), ALU.is_equal))
            for i in range(TILES):
                ins = V.tensor_tensor(t32[:, i, :].rearrange("p (g e) -> p g e", e=NE), lg[:, i, NG:LW].rearrange("p (g e) -> p g e", e=NE),
                                      ohg[:, i, :].unsqueeze(2).to_broadcast([P, NG, NE]), ALU.mult)
            own(ins)
            for i in range(TILES):
                ins = V.tensor_reduce(le[:, i, :], t32[:, i, :].rearrange("p (g e) -> p e g", e=NE), AX, ALU.add)
            own(ins)
            for i in range(TILES):
                ins = V.max(lm[:, i, :], le[:, i, :])
            own(ins)
            for i in range(TILES):
                ins = V.max_index(li[:, i, :], lm[:, i, :], le[:, i, :])
            own(ins)
            at = lambda x, n: x[:, :, n:n + 1].rearrange("p i a -> p (i a)")
            own(V.tensor_tensor(f[:, 0, :], at(lm, 1), at(lm, 0), ALU.subtract))
            dve.sem_inc(ex_in, 1)
            dve.wait_ge(ex_out, 2)
            own(V.tensor_scalar(f[:, 4, :], f[:, 1, :], 1.0, None, ALU.add))
            own(V.reciprocal(f[:, 4, :], f[:, 4, :]))
            own(V.tensor_tensor(f[:, 4, :], f[:, 4, :], f[:, 2, :], ALU.mult))
            own(V.tensor_copy(m.wt[:, :, 0:1].rearrange("p i a -> p (i a)"), f[:, 4, :]))
            own(V.tensor_tensor(m.wt[:, :, 1:2].rearrange("p i a -> p (i a)"), f[:, 4, :], f[:, 1, :], ALU.mult))
            for c in range(TOPK):
                own(V.tensor_copy(f[:, 5 + c, :], at(li, c)))
                own(V.scalar_tensor_tensor(f[:, 5 + c, :], f[:, 3, :], float(NE), f[:, 5 + c, :], ALU.mult, ALU.add))
                own(V.tensor_tensor(oh[:, c, :, :], iota[:, :].unsqueeze(1).to_broadcast([P, TILES, EXPERTS]),
                                    f[:, 5 + c, :].unsqueeze(2).to_broadcast([P, TILES, EXPERTS]), ALU.is_equal))
                own(V.tensor_tensor(oh[:, c, :, :], oh[:, c, :, :], valid[:, :].unsqueeze(2).to_broadcast([P, TILES, EXPERTS]), ALU.mult))
            own(V.tensor_tensor(oh[:, 2, :, :], oh[:, 0, :, :], oh[:, 1, :, :], ALU.add))
            dve.sem_inc(oh_ok, 1)
            dve.wait_ge(rank_pe, 1)
            dve.wait_ge(rank_in, 16)
            n_e, more, upto, base = (cnt[:, k, :] for k in range(4))
            own(V.tensor_copy(n_e, m.banks[1][:, 0:EXPERTS]))
            big = junk[:, 3 * TILES * EXPERTS:3 * TILES * EXPERTS + EXPERTS * MORE].rearrange("p (e k) -> p e k", k=MORE)
            own(V.tensor_tensor(big, n_e.unsqueeze(2).to_broadcast([P, EXPERTS, MORE]),
                                steps.unsqueeze(1).to_broadcast([P, EXPERTS, MORE]), ALU.is_gt))
            own(V.tensor_reduce(more, big, AX, ALU.add))
            own(V.tensor_tensor_scan(upto, rankc[:, P:P + EXPERTS], more, float(EXPERTS), ALU.mult, ALU.add))
            own(V.tensor_tensor(base, upto, more, ALU.subtract))
            for c in range(TOPK):
                rank, q, z, blk, at0 = (f[:, k, :] for k in (7, 8, 9, 10, 11))
                e = f[:, 5 + c, :]
                own(V.tensor_tensor(t32, oh[:, c, :, :], m.banks[0][:, 0:TILES * EXPERTS].rearrange("p (i e) -> p i e", e=EXPERTS), ALU.mult))
                own(V.tensor_reduce(rank, t32, AX, ALU.add))
                own(V.tensor_tensor(t32, oh[:, c, :, :], base.unsqueeze(1).to_broadcast([P, TILES, EXPERTS]), ALU.mult))
                own(V.tensor_reduce(at0, t32, AX, ALU.add))
                own(V.tensor_tensor(past, rank.unsqueeze(2).to_broadcast([P, TILES, MORE]),
                                    steps.unsqueeze(1).to_broadcast([P, TILES, MORE]), ALU.is_ge))
                own(V.tensor_reduce(q, past, AX, ALU.add))
                own(V.tensor_scalar(z, q, 1.0, None, ALU.min))
                own(V.scalar_tensor_tensor(blk, at0, -1.0, q, ALU.add, ALU.add))
                own(V.tensor_tensor(blk, blk, e, ALU.subtract))
                own(V.tensor_tensor(blk, blk, z, ALU.mult))
                own(V.tensor_tensor(blk, blk, e, ALU.add))
                own(V.scalar_tensor_tensor(rank, q, -float(SLOTS), rank, ALU.mult, ALU.add))
                own(V.scalar_tensor_tensor(f[:, 12, :], rank, float(BLOCKS), blk, ALU.mult, ALU.add))
                own(V.scalar_tensor_tensor(f[:, 13, :], blk, float(SLOTS), rank, ALU.mult, ALU.add))
                own(V.tensor_copy(post[:, :, c:c + 1].rearrange("p i a -> p (i a)"), f[:, 12, :]))
                dve.sem_inc(pos_ok, 1)
                own(V.tensor_copy(m.posy[:, :, c:c + 1].rearrange("p i a -> p (i a)"), f[:, 13, :]))
            assert OVER == 2 * OWN
            for j in (0, OWN):
                own(V.tensor_tensor(own32, upto[0:1, :].unsqueeze(1).to_broadcast([1, OWN, EXPERTS]),
                                    later[:, j:j + OWN].unsqueeze(2).to_broadcast([1, OWN, EXPERTS]), ALU.is_le))
                own(V.tensor_reduce(m.ownf[:, j:j + OWN], own32, AX, ALU.add))
            own(V.tensor_scalar(m.ownf[:, 0:OVER], m.ownf[:, 0:OVER], float(EXPERTS - 1), None, ALU.min))
            own(V.tensor_scalar(m.ownf[:, OVER:OVER + 1], upto[0:1, EXPERTS - 1:EXPERTS], -float(EXPERTS), None, ALU.add))
            own(V.tensor_copy(m.owni[:], m.ownf[:]))


def phase_e(nc, I, O, m):
    with ExitStack() as ctx:
        sb = lambda name, shape, dt=F32: ctx.enter_context(nc.sbuf_tensor(name, shape, dt))
        sem = lambda name: ctx.enter_context(nc.semaphore("e_" + name))
        DOWN = 2 * HID * KD
        tab = sb("slot_rows", [SLOTS, BLOCKS], I32)
        idx = sb("row_now", [SLOTS, 2, 1], I32)
        pad = sb("unread", [SLOTS, 1, 1], I32)
        hg = sb("rows", [SLOTS, 2, D])
        hgT = sb("rows_t", [P, KD, SLOTS])
        ac = sb("act", [P, 2, 2, HID // 2])
        acT = sb("act_t", [P, HID // P, SLOTS])
        assert 2 * SLOTS == P and HID == 2 * P
        y = sb("y_buf", [P, 2, D // 2])
        tab_in = sem("table")

        def sems(tag):
            names = ("idx", "gathered0", "gathered1", "turned", "tT_dve", "tT_act", "gu", "exp", "act", "act_turned", "actT", "down", "y_act", "stored0", "stored1", "dve_own")
            return {n: sem(tag + n) for n in names}
        S, X = sems("main_"), sems("more_")
        win = m.w_in
        xw = sem("more_w")
        block = ctx.enter_context(nc.Block(no_gpsimd_drain=True))

        def at_least(eng, s, value):
            if not isinstance(value, int) or value > 0:
                eng.wait_ge(s, value)

        class Turn:

            def __init__(self, i, off):
                self.n, self.p, self.u = i * RING + off, off % 2, off % RING
                self.two_back = i * RING + off - 1
                self.half, self.round = i * (RING // 2) + off // 2, i + off // RING

        class Single:

            def __init__(self, j):
                self.n = self.half = self.round = self.two_back = j
                self.p = self.u = 0

        def gather(pool, s, t, col):
            b, p = t.n, t.p
            at_least(pool, s["turned"], t.two_back)
            nc.gpsimd.tensor_copy(idx[:, p, :], tab[:, ds(col, 1)]).then_inc(s["idx"], 1)
            pool.wait_ge(s["idx"], 2 * b + 1)
            nc.gpsimd.tensor_tensor(pad[:, 0, :], tab[:, 0:1], tab[:, 0:1], ALU.add).then_inc(s["idx"], 1)
            pool.indirect_dma_start(out=hg[:, p, :], out_offset=None, in_=m.h2,
                                    in_offset=bass.IndirectOffsetOnAxis(ap=idx[:, p, :], axis=0)).then_inc(s[f"gathered{p}"], 16)

        def turn(pe, s, t):
            b, p = t.n, t.p
            pe.wait_ge(s[f"gathered{p}"], t.half * 16 + 16)
            at_least(pe, s["tT_dve"], b)
            at_least(pe, s["tT_act"], b)
            nc.tensor.transpose(m.banks[7][:, 0:P], m.ident[:, :], m.ident[:, :])
            for k in range(KD):
                mm = nc.tensor.transpose(m.banks[k // 4][:, (k % 4) * SLOTS:(k % 4 + 1) * SLOTS], hg[:, p, k * P:(k + 1) * P],
                                         m.ident[0:SLOTS, 0:SLOTS])
            mm.then_inc(s["turned"], 1)

        def gate_up(pe, s, t, arrived):
            b, p, u = t.n, t.p, t.u
            pe.wait_ge(s["tT_dve"], b + 1)
            pe.wait_ge(s["tT_act"], b + 1)
            pe.wait_ge(arrived, t.round * 16 + 16)
            at_least(pe, s["act"], t.two_back)
            for k in range(KD):
                for x in range(2):
                    mm = nc.tensor.matmul(m.banks[2 + p][x * SLOTS:(x + 1) * SLOTS, 0:HID], hgT[:, k, :],
                                          m.weights(u)[:, (2 * k + x) * HID:(2 * k + x + 1) * HID], start=k == 0, stop=k == KD - 1)
            mm.then_inc(s["gu"], 1)

        def turn_act(pe, s, t):
            b, p = t.n, t.p
            pe.wait_ge(s["act"], b + 1)
            at_least(pe, s["actT"], b)
            nc.tensor.transpose(m.banks[4][:, 0:P], ac[:, p, 1, :], m.ident[:, :]).then_inc(s["act_turned"], 1)

        def down(pe, s, t):
            b, p, u = t.n, t.p, t.u
            pe.wait_ge(s["actT"], b + 1)
            at_least(pe, s["y_act"], t.two_back)
            for k in range(HID // P):
                for x in range(2):
                    c = DOWN + k * D + x * 512
                    mm = nc.tensor.matmul(m.banks[5 + p][x * SLOTS:(x + 1) * SLOTS, :], acT[:, k, :], m.weights(u)[:, c:c + 512],
                                          start=k == 0, stop=k == HID // P - 1)
            mm.then_inc(s["down"], 1)

        def rows_out(eng, copy, s, t, x, name):
            b = t.n
            eng.wait_ge(s["turned"], b + 1)
            at_least(eng, s["gu"], b)
            copy(hgT[:, 4 * x:4 * x + 4, :], m.banks[x][:, 0:4 * SLOTS].rearrange("p (k r) -> p k r", r=SLOTS)).then_inc(s[name], 1)

        def act_exp(s, act, t):
            b, p = t.n, t.p
            act.wait_ge(s["gu"], b + 1)
            at_least(act, s["act_turned"], t.two_back)
            nc.scalar.activation(ac[:, p, 0, :], m.banks[2 + p][:, 0:P], ACT.Exp, scale=-1.0).then_inc(s["exp"], 1)

        def act_mul(s, dve, t, own):
            b, p = t.n, t.p
            own.n, own.loop = 0, b * 3
            dve.wait_ge(s["exp"], b + 1)
            a, o = ac[:, p, 0, :], ac[:, p, 1, :]
            own(nc.vector.tensor_scalar(a, a, 1.0, None, ALU.add))
            own(nc.vector.reciprocal(a, a))
            own(nc.vector.tensor_tensor(a, m.banks[2 + p][:, 0:P], a, ALU.mult))
            nc.vector.tensor_tensor(o, m.banks[2 + p][:, P:2 * P], a, ALU.mult).then_inc(s["act"], 1)

        def actT_out(s, dve, t):
            b = t.n
            dve.wait_ge(s["act_turned"], b + 1)
            at_least(dve, s["down"], b)
            nc.vector.tensor_copy(acT[:, :, :].rearrange("p k r -> p (k r)"), m.banks[4][:, 0:HID // P * SLOTS]).then_inc(s["actT"], 1)

        def y_out(s, act, t):
            b, p = t.n, t.p
            act.wait_ge(s["down"], b + 1)
            at_least(act, s[f"stored{p}"], t.half * 32)
            nc.scalar.activation(y[:, p, :], m.banks[5 + p][:, :], ACT.Copy).then_inc(s["y_act"], 1)

        def store(sp, s, t, row):
            b, p = t.n, t.p
            sp.wait_ge(s["y_act"], b + 1)
            for x in range(2):
                sp.dma_start(m.y[ds(row * SLOTS, SLOTS), x * 512:(x + 1) * 512], y[x * SLOTS:(x + 1) * SLOTS, p, :]).then_inc(s[f"stored{p}"], 16)

        def pipeline(eng, step):
            def at(i, off):
                step(*(Turn(i, off - d) if not isinstance(i, int) or 0 <= off - d < EXPERTS else None for d in range(3)))
            for u in range(RING):
                at(0, u)
            with eng.Fori(1, EXPERTS // RING) as i:
                for u in range(RING):
                    at(i, u)
            at(0, EXPERTS)
            at(0, EXPERTS + 1)

        def further(eng, body, after=None):
            n = eng.value_load(m.owni[0:1, OVER:OVER + 1], min_val=0, max_val=OVER)
            with eng.If(n > 0):
                with eng.Fori(0, n) as j:
                    body(j)
                if after:
                    after(n)

        def further_in(sp, j):
            e = sp.value_load(m.owni[0:1, ds(j, 1)], min_val=0, max_val=EXPERTS - 1)
            sp.dma_start(m.weights(0), I["w_exp"][ds(e, 1)].rearrange("a p n -> (a p) n")).then_inc(xw, 16)

        @block.sync
        def _(sp):
            sp.dma_start(tab[:], m.table).then_inc(tab_in, 16)
            with sp.Fori(0, EXPERTS // RING - 1) as i:
                for u in range(RING):
                    t = Turn(i, u)
                    sp.wait_ge(S["down"], t.n + 1)
                    sp.dma_start(m.weights(u), I["w_exp"][ds(t.n + RING, 1)].rearrange("a p n -> (a p) n")).then_inc(win[u], 16)
                    store(sp, S, t, t.n)
            n = sp.value_load(m.owni[0:1, OVER:OVER + 1], min_val=0, max_val=OVER)
            sp.wait_ge(S["down"], EXPERTS - RING + 1)
            with sp.If(n > 0):
                further_in(sp, 0)
            for b in range(EXPERTS - RING, EXPERTS):
                store(sp, S, Turn(0, b), b)
            sp.wait_ge(S["stored0"], 32 * EXPERTS // 2)
            sp.wait_ge(S["stored1"], 32 * EXPERTS // 2)
            with sp.If(n > 0):
                store(sp, X, Single(0), EXPERTS)
            with sp.If(n > 1):
                with sp.Fori(1, n) as j:
                    sp.wait_ge(X["down"], j)
                    further_in(sp, j)
                    store(sp, X, Single(j), j + EXPERTS)

        @block.gpsimd
        def _(pool):
            pool.wait_ge(tab_in, 16)
            for u in range(RING):
                gather(pool, S, Turn(0, u), u)
            with pool.Fori(1, EXPERTS // RING) as i:
                for u in range(RING):
                    gather(pool, S, Turn(i, u), i * RING + u)
            pool.wait_ge(S["turned"], EXPERTS)
            pool.wait_ge(S["idx"], 2 * EXPERTS)

            def body(j):
                at_least(pool, X["stored0"], j * 32)
                gather(pool, X, Single(j), j + EXPERTS)
                pool.wait_ge(X["idx"], j * 2 + 2)
                pool.wait_ge(X["gathered0"], j * 16 + 16)
            further(pool, body, lambda n: pool.wait_ge(X["stored0"], n * 32))

        @block.tensor
        def _(pe):
            def step(t, before, third):
                if before:
                    gate_up(pe, S, before, win[before.u])
                if third:
                    turn_act(pe, S, third)
                if t:
                    turn(pe, S, t)
                if third:
                    down(pe, S, third)
            pipeline(pe, step)

            def body(j):
                t = Single(j)
                at_least(pe, X["stored0"], j * 32)
                turn(pe, X, t)
                gate_up(pe, X, t, xw)
                turn_act(pe, X, t)
                down(pe, X, t)
            further(pe, body)

        @block.scalar
        def _(act):
            copy = lambda o, i: nc.scalar.activation(o, i, ACT.Copy)

            def step(t, before, third):
                if before:
                    act_exp(S, act, before)
                if t:
                    rows_out(act, copy, S, t, 1, "tT_act")
                if third:
                    y_out(S, act, third)
            pipeline(act, step)
            act.wait_ge(S["stored0"], 32 * EXPERTS // 2)

            def body(j):
                t = Single(j)
                rows_out(act, copy, X, t, 1, "tT_act")
                act_exp(X, act, t)
                y_out(X, act, t)
            further(act, body)

        @block.vector
        def _(dve):
            copy = lambda o, i: nc.vector.tensor_copy(o, i)
            own, more_own = Link(dve, S["dve_own"]), Link(dve, X["dve_own"])

            def step(t, before, third):
                if third:
                    actT_out(S, dve, third)
                if t:
                    rows_out(dve, copy, S, t, 0, "tT_dve")
                if before:
                    act_mul(S, dve, before, own)
            pipeline(dve, step)

            def body(j):
                t = Single(j)
                rows_out(dve, copy, X, t, 0, "tT_dve")
                act_mul(X, dve, t, more_own)
                actT_out(X, dve, t)
            further(dve, body)


def phase_f(nc, I, O, m):
    with ExitStack() as ctx:
        sb = lambda name, shape, dt=F32: ctx.enter_context(nc.sbuf_tensor(name, shape, dt))
        sem = lambda name: ctx.enter_context(nc.semaphore("f_" + name))
        got = m.w[:, 0:TOPK * TILES * D].rearrange("p (c i n) -> p c i n", c=TOPK, i=TILES)
        gain = sb("gain_ffn", [P, D])
        junk = sb("f_squares", [P, D])
        ss = sb("f_sums", [P, 4, TILES])
        gain_in, spread, spread_out, picked, summed, sq, rq, rs, done, stored, dve_own, act_own = [sem(n) for n in (
            "gain", "spread", "spread_out", "picked", "summed", "squares", "mean", "rstd", "rows_done", "stored", "dve_own", "act_own")]
        each = [sem(f"picked{i}") for i in range(TILES)]
        block = ctx.enter_context(nc.Block(no_gpsimd_drain=True))
        spread_pe, spread_dve, SPREAD = spread_steps(m, [(2, 10, gain)], spread, spread_out)

        @block.sync
        def _(sp):
            sp.dma_start(gain[:], I["g_post_ffn"].partition_broadcast(P)).then_inc(gain_in, 16)
            for i in range(TILES):
                sp.wait_ge(done, i + 1)
                dst = O["y_prompt"][i * P:(i + 1) * P, :] if i < TILES - 1 else O["y_sample"]
                sp.dma_start(dst, m.x1[0:ROWS[i], i, :]).then_inc(stored, 16)
            sp.wait_ge(stored, 16 * TILES)
            sp.wait_ge(m.s_keep, 16 * GROUPS * NSEQ)

        @block.gpsimd
        def _(pool):
            for i in range(TILES):
                for c in range(TOPK):
                    pool.indirect_dma_start(out=got[0:ROWS[i], c, i, :], out_offset=None, in_=m.y,
                                            in_offset=bass.IndirectOffsetOnAxis(ap=m.posy[0:ROWS[i], i, c:c + 1], axis=0)).then_inc(each[i], 16)

        @block.tensor
        def _(pe):
            spread_pe(nc, pe)

        @block.scalar
        def _(act):
            own = Link(act, act_own)
            for i in range(TILES):
                r = slice(0, ROWS[i])
                act.wait_ge(summed, i + 1)
                own(nc.scalar.activation(junk[r, :], got[r, 0, i, :], ACT.Square, accum_out=ss[r, 0, i:i + 1]))
                act.sem_inc(sq, 1)
                act.wait_ge(rq, i + 1)
                own(nc.scalar.activation(ss[r, 2, i:i + 1], ss[r, 1, i:i + 1], ACT.Ln))
                nc.scalar.activation(ss[r, 3, i:i + 1], ss[r, 2, i:i + 1], ACT.Exp, scale=-0.5).then_inc(rs, 1)

        @block.vector
        def _(dve):
            own = Link(dve, dve_own)
            dve.wait_ge(gain_in, 16)
            spread_dve(nc, dve)
            dve.wait_ge(spread_out, SPREAD)

            def finish(i):
                r = slice(0, ROWS[i])
                dve.wait_ge(rs, i + 1)
                own(nc.vector.scalar_tensor_tensor(got[r, 0, i, :], got[r, 0, i, :], ss[r, 3, i:i + 1], scale_of(m, i, 2)[r],
                                                   ALU.mult, ALU.mult))
                nc.vector.tensor_tensor(m.x1[r, i, :], m.x1[r, i, :], got[r, 0, i, :], ALU.add).then_inc(done, 1)

            for i in range(TILES + 1):
                if i < TILES:
                    r = slice(0, ROWS[i])
                    dve.wait_ge(each[i], 16 * TOPK)
                    own(nc.vector.tensor_scalar(got[r, 0, i, :], got[r, 0, i, :], m.wt[r, i, 0:1], None, ALU.mult))
                    nc.vector.scalar_tensor_tensor(got[r, 0, i, :], got[r, 1, i, :], m.wt[r, i, 1:2], got[r, 0, i, :],
                                                   ALU.mult, ALU.add).then_inc(summed, 1)
                if i >= 1:
                    finish(i - 1)
                if i < TILES:
                    dve.wait_ge(sq, i + 1)
                    nc.vector.tensor_scalar(ss[r, 1, i:i + 1], ss[r, 0, i:i + 1], 1.0 / D, EPS, ALU.mult, ALU.add).then_inc(rq, 1)


def kernel(**inputs):
    import concourse.bacc as bacc
    from concourse.bass_utils import run_bass_kernel_spmd as run

    a = {k: np.asarray(v) for k, v in inputs.items()}
    c = np.ascontiguousarray

    def tiles(w, parts):
        k, n = w.shape
        w = w.reshape(k // P, P, parts, n // parts)
        return c(w.transpose(2, 1, 0, 3)).reshape(parts, P, -1)

    cond = np.zeros((32, D), np.float32)
    cond[0], cond[1:1 + NSEQ] = a["c_prompt"][0], a["c_sample"]
    w_in = a["w_in"][0]
    gates = w_in[:, QKV:]
    weg, weu, wed = (a[n][0].reshape(EXPERTS, *a[n].shape[-2:]) for n in ("w_exp_gate", "w_exp_up", "w_exp_down"))
    gu = np.stack([weg.reshape(EXPERTS, KD, P, 2, HID // 2), weu.reshape(EXPERTS, KD, P, 2, HID // 2)], axis=4)
    gu = gu.transpose(0, 2, 1, 3, 4, 5).reshape(EXPERTS, P, -1)
    down = wed.reshape(EXPERTS, HID // P, P, D).transpose(0, 2, 1, 3).reshape(EXPERTS, P, -1)
    ins = {
        "x_prompt": a["x_prompt"][0], "x_sample": a["x_sample"].reshape(NS, D),
        "cond": cond.reshape(32, KD, P).transpose(2, 1, 0),
        "w_ada": tiles(a["w_ada"][0], ADA),
        "b_ada": a["b_ada"][0].reshape(ADA // 4, 4, 512).transpose(1, 0, 2),
        "w_qkv": tiles(w_in[:, :QKV], CH), "w_gates": tiles(gates, 4), "b_f": a["b_f"][0],
        "g_pre_mix": a["g_pre_mix"][0], "g_post_mix": a["g_post_mix"][0],
        "g_pre_ffn": a["g_pre_ffn"][0], "g_post_ffn": a["g_post_ffn"][0],
        "w_pa": tiles(a["w_pa"][0], 1)[0], "w_pb": tiles(a["w_pb"][0], 1)[0], "w_o": tiles(a["w_o"][0], 1)[0],
        "w_r": tiles(np.concatenate([a["w_router_group"][0], a["w_router_expert"][0].transpose(1, 0, 2).reshape(D, EXPERTS)], axis=1), 1)[0],
        "b_r": np.concatenate([a["b_router_group"][0], a["b_router_expert"][0].reshape(-1)]),
        "w_exp": np.concatenate([gu, down], axis=2),
        "page_table": a["page_table"].reshape(1, -1).astype(np.int32),
        "cache_b_k": a["cache_b_k"][0].reshape(POOL, PAGE, BW), "cache_b_v": a["cache_b_v"][0].reshape(POOL, PAGE, BW),
        "cache_b_logf": a["cache_b_logf"][0].reshape(POOL, PAGE * BH),
        **{f"cache_a{g + 1}": a[f"cache_a{g + 1}_kv"][0].reshape(NSEQ, BUFROWS[g], -1) for g in range(GROUPS)},
        **constants(),
    }
    KVW = 2 * AH * HD
    outs = {
        "y_prompt": (SEQ, D), "y_sample": (NS, D),
        **{f"a{g + 1}_prompt": (min(WIN[g], SEQ), KVW) for g in range(GROUPS)},
        **{f"a{g + 1}_sample": (NSEQ, BUFROWS[g], KVW) for g in range(GROUPS)},
        "bk_prompt": (SEQ, BW), "bk_sample": (NS, BW), "bv_prompt": (SEQ, BW), "bv_sample": (NS, BW),
        "blogf_prompt": (SEQ, BH), "blogf_sample": (NS, BH),
    }
    nc = bacc.Bacc("TRN2", target_bir_lowering=False, num_devices=1)
    arrays, I, O = {}, {}, {}
    for name, arr in ins.items():
        arrays["in_" + name] = arr = c(arr)
        I[name] = nc.dram_tensor("in_" + name, arr.shape, mybir.dt.from_np(arr.dtype), kind="ExternalInput").ap()
    for name, shape in outs.items():
        O[name] = nc.dram_tensor("out_" + name, shape, F32, kind="ExternalOutput").ap()
    build(nc, I, O)
    r = run(nc, [arrays], core_ids=[0]).results[0]
    got = {name: r["out_" + name] for name in outs}

    def kv(name, *lead):
        return got[name].reshape(1, *lead, 2, AH, HD)

    return (
        got["y_prompt"].reshape(1, SEQ, D), got["y_sample"].reshape(NSEQ, DEC, D),
        *[z for g in range(GROUPS) for z in (kv(f"a{g + 1}_prompt", 1, min(WIN[g], SEQ)),
                                             kv(f"a{g + 1}_sample", NSEQ, BUFROWS[g]))],
        got["bk_prompt"].reshape(1, 1, SEQ, BH, HD), got["bk_sample"].reshape(1, NSEQ, DEC, BH, HD),
        got["bv_prompt"].reshape(1, 1, SEQ, BH, HD), got["bv_sample"].reshape(1, NSEQ, DEC, BH, HD),
        got["blogf_prompt"].reshape(1, 1, SEQ, BH), got["blogf_sample"].reshape(1, NSEQ, DEC, BH),
    )
```
